# Optimizing a Trainium2 kernel written in Bass

```python
import jax
import jax.numpy as jnp
from jax import lax
import numpy as np

D_MODEL = 1024
BATCH = 1
SEQ = 256
DEPTH = 2

CHUNK = 64
ROPE_THETA = 10000.0
NORM_EPS = 1e-6
QUERY_BLOCK = 128

A_HEADS = 4
A_DK = 128
A_DV = 128
A_KEY = A_HEADS * A_DK
A_WIDTH = A_HEADS * A_DV
B_HEADS = 8
B_KV_HEADS = 2
B_HD = 64
B_WINDOW = 128
B_WINDOW_CHUNKS = B_WINDOW // CHUNK
B_WIDTH = B_HEADS * B_HD
C_HEADS = 8
C_HD = 64
C_WIDTH = C_HEADS * C_HD
C_TOPK_MAX = 256
IDX_HEADS = 4
IDX_HD = 64
N_BRANCHES = 3
N_EXPERTS = 32
N_GROUPS = 8
EXPERTS_PER_GROUP = N_EXPERTS // N_GROUPS
GROUP_SCORE_TOPK = 2
TOP_K = 2
D_FF_EXPERT = 256

IN_SIZES = (A_KEY, A_KEY, A_WIDTH, A_WIDTH,
            B_WIDTH, B_KV_HEADS * B_HD, B_KV_HEADS * B_HD,
            C_WIDTH, C_HD, C_HD,
            IDX_HEADS * IDX_HD, IDX_HD, IDX_HEADS,
            N_BRANCHES * D_MODEL)
N_IN = sum(IN_SIZES)

kernel_name = 'hybrid_hgrn2_swa_dsa_grouped_moe_adaln'

F32 = jnp.float32

def rms_norm(x, g):
    xf = x.astype(F32)
    y = xf * lax.rsqrt(jnp.mean(xf * xf, -1, keepdims=True) + NORM_EPS)
    return (y * g.astype(F32)).astype(x.dtype)

def rope(x, pos):
    hd = x.shape[-1]
    half = hd // 2
    inv_freq = ROPE_THETA ** (-jnp.arange(half, dtype=F32) * 2.0 / hd)
    ang = pos.astype(F32)[..., None] * inv_freq
    cos = jnp.cos(ang)[:, :, None, :]
    sin = jnp.sin(ang)[:, :, None, :]
    xf = x.astype(F32)
    x1, x2 = xf[..., :half], xf[..., half:]
    return jnp.concatenate([x1 * cos - x2 * sin, x2 * cos + x1 * sin], -1).astype(x.dtype)

def hgrn2_mixer(q_raw, f_raw, i_val, g_out, lower_bound, norm_g):
    bn, s_len, _ = q_raw.shape
    nc = s_len // CHUNK
    f = lower_bound + (1.0 - lower_bound) * jax.nn.sigmoid(f_raw.astype(F32))
    log_f = jnp.log(f)
    k = 1.0 - f
    q = jax.nn.silu(q_raw.astype(F32))

    def to_chunks(t, d):
        return t.reshape(bn, nc, CHUNK, A_HEADS, d).transpose(1, 0, 3, 2, 4)

    qs, ks, gs = to_chunks(q, A_DK), to_chunks(k, A_DK), to_chunks(log_f, A_DK)
    vs = to_chunks(i_val.astype(F32), A_DV)
    causal = jnp.tril(jnp.ones((CHUNK, CHUNK), bool))

    def step(state, inp):
        qc, kc, gc, vc = inp
        b = jnp.cumsum(gc, axis=2)
        b_last = b[:, :, -1:, :]
        inter = jnp.einsum('bhtk,bhkv->bhtv', qc * jnp.exp(b), state)
        diff = b[:, :, :, None, :] - b[:, :, None, :, :]
        decay = jnp.exp(jnp.where(causal[:, :, None], diff, -jnp.inf))
        scores = jnp.sum(qc[:, :, :, None, :] * decay * kc[:, :, None, :, :], -1)
        intra = jnp.einsum('bhts,bhsv->bhtv', scores, vc)
        new_state = (state * jnp.exp(b_last)[:, :, 0, :, None]
                     + jnp.einsum('bhsk,bhsv->bhkv', kc * jnp.exp(b_last - b), vc))
        return new_state, inter + intra

    s0 = jnp.zeros((bn, A_HEADS, A_DK, A_DV), F32)
    _, o = lax.scan(step, s0, (qs, ks, gs, vs))
    o = o.transpose(1, 0, 3, 2, 4).reshape(bn, s_len, A_HEADS, A_DV)
    o = o * lax.rsqrt(jnp.mean(o * o, -1, keepdims=True) + NORM_EPS) * norm_g.astype(F32).reshape(A_HEADS, A_DV)
    o = o.reshape(bn, s_len, A_WIDTH) * jax.nn.silu(g_out.astype(F32))
    return o.astype(q_raw.dtype)

def swa_sink_mixer(q, k, v, sinks):
    bn, s_len = q.shape[:2]
    nc = s_len // CHUNK
    grp = B_HEADS // B_KV_HEADS
    qb = q.reshape(bn, nc, CHUNK, B_KV_HEADS, grp, B_HD)
    shifts = list(range(B_WINDOW_CHUNKS - 1, -1, -1))

    def band(t):
        tb = t.reshape(bn, nc, CHUNK, B_KV_HEADS, B_HD)
        parts = [jnp.pad(tb, ((0, 0), (j, 0), (0, 0), (0, 0), (0, 0)))[:, :nc] for j in shifts]
        return jnp.concatenate(parts, axis=2)

    kb, vb = band(k), band(v)
    chunk_ids = jnp.arange(nc)
    valid = jnp.concatenate([jnp.broadcast_to((chunk_ids >= j)[:, None], (nc, CHUNK)) for j in shifts], axis=1)
    scores = jnp.einsum('bnqkgd,bnskd->bnkgqs', qb, kb).astype(F32) * (B_HD ** -0.5)
    scores = jnp.where(valid[None, :, None, None, None, :], scores, -jnp.inf)
    sink = sinks.astype(F32).reshape(1, 1, B_KV_HEADS, grp, 1, 1)
    m = jnp.maximum(jnp.max(scores, -1, keepdims=True), sink)
    p = jnp.exp(scores - m)
    probs = p / (jnp.sum(p, -1, keepdims=True) + jnp.exp(sink - m))
    out = jnp.einsum('bnkgqs,bnskd->bnqkgd', probs.astype(v.dtype), vb)
    return out.reshape(bn, s_len, B_WIDTH)

def dsa_mixer(q, k, v, iq, ik, iw):
    bn, s_len = q.shape[:2]
    topk = min(C_TOPK_MAX, s_len // 4)
    nqb = s_len // QUERY_BLOCK
    key_chunk = jnp.arange(s_len) // CHUNK
    starts = jnp.arange(nqb) * QUERY_BLOCK
    gather = jax.vmap(lambda table, idx: table[idx])

    def blocks(t):
        return t.reshape((bn, nqb, QUERY_BLOCK) + t.shape[2:]).swapaxes(0, 1)

    def attend_block(args):
        qb, iqb, iwb, start = args
        q_chunk = (start + jnp.arange(QUERY_BLOCK)) // CHUNK
        admissible = key_chunk[None, :] <= q_chunk[:, None]
        logits = jnp.einsum('bqhd,bsd->bqhs', iqb, ik).astype(F32)
        idx_score = jnp.einsum('bqhs,bqh->bqs', jax.nn.relu(logits), iwb.astype(F32))
        idx_score = jnp.where(admissible[None], idx_score, -jnp.inf)
        _, sel = lax.top_k(idx_score, topk)
        sel_valid = key_chunk[sel] <= q_chunk[None, :, None]
        k_sel = gather(k, sel)
        v_sel = gather(v, sel)
        s = jnp.einsum('bqhd,bqjd->bhqj', qb, k_sel).astype(F32) * (C_HD ** -0.5)
        s = jnp.where(sel_valid[:, None], s, -jnp.inf)
        p = jax.nn.softmax(s, axis=-1)
        return jnp.einsum('bhqj,bqjd->bqhd', p.astype(v.dtype), v_sel)

    out = lax.map(attend_block, (blocks(q), blocks(iq), blocks(iw), starts))
    return out.swapaxes(0, 1).reshape(bn, s_len, C_WIDTH)

def mixer_block(h, pos, w_in, lower_bound, hgrn_norm_g, sinks, w_branch_a, w_branch_b, w_branch_c, w_out):
    bn, s_len, _ = h.shape
    proj = h @ w_in
    offsets = np.cumsum(IN_SIZES)[:-1].tolist()
    (a_q, a_f, a_i, a_g, b_q, b_k, b_v, c_q, c_k, c_v,
     i_q, i_k, i_w, gate_logits) = jnp.split(proj, offsets, axis=-1)

    def heads(t, n):
        return t.reshape(bn, s_len, n, -1)

    y_a = hgrn2_mixer(a_q, a_f, a_i, a_g, lower_bound, hgrn_norm_g)
    y_b = swa_sink_mixer(rope(heads(b_q, B_HEADS), pos), rope(heads(b_k, B_KV_HEADS), pos),
                         heads(b_v, B_KV_HEADS), sinks)
    y_c = dsa_mixer(rope(heads(c_q, C_HEADS), pos), rope(heads(c_k, 1), pos)[:, :, 0], c_v,
                    rope(heads(i_q, IDX_HEADS), pos), rope(heads(i_k, 1), pos)[:, :, 0], i_w)
    gates = jax.nn.sigmoid(gate_logits.astype(F32)).reshape(bn, s_len, N_BRANCHES, D_MODEL).astype(h.dtype)
    merged = (gates[:, :, 0] * (y_a @ w_branch_a)
              + gates[:, :, 1] * (y_b @ w_branch_b)
              + gates[:, :, 2] * (y_c @ w_branch_c))
    return merged @ w_out

def moe_ffn(h, router_w, router_b, w_gate, w_up, w_down):
    bn, s_len, d = h.shape
    t = h.reshape(bn * s_len, d)
    affinity = jax.nn.sigmoid((t @ router_w).astype(F32))
    biased = (affinity + router_b.astype(F32)).reshape(-1, N_GROUPS, EXPERTS_PER_GROUP)
    group_score = jnp.sum(lax.top_k(biased, GROUP_SCORE_TOPK)[0], -1)
    best_group = jnp.argmax(group_score, -1)
    in_group = jnp.take_along_axis(biased, best_group[:, None, None], axis=1)[:, 0]
    _, local = lax.top_k(in_group, TOP_K)
    expert_idx = best_group[:, None] * EXPERTS_PER_GROUP + local
    w = jnp.take_along_axis(affinity, expert_idx, axis=1)
    w = w / jnp.sum(w, -1, keepdims=True)
    combine = jnp.einsum('nk,nke->ne', w, jax.nn.one_hot(expert_idx, N_EXPERTS, dtype=F32)).astype(h.dtype)
    y = jnp.zeros_like(t)
    for e in range(N_EXPERTS):
        he = jax.nn.silu(t @ w_gate[e]) * (t @ w_up[e])
        y = y + combine[:, e:e + 1] * (he @ w_down[e])
    return y.reshape(bn, s_len, d)

def setup_inputs(seed: int = 0) -> dict:
    key = jax.random.key(seed)
    ks = jax.random.split(key, 24)

    def nrm(k, shape, scale):
        return jax.random.normal(k, shape, F32) * scale

    x = nrm(ks[0], (BATCH, SEQ, D_MODEL), 1.0)
    c = nrm(ks[1], (BATCH, D_MODEL), 1.0)
    positions = (jax.random.randint(ks[2], (BATCH, 1), 0, 4096, dtype=jnp.int32)
                 + jnp.arange(SEQ, dtype=jnp.int32)[None, :])
    return {
        'x': x,
        'c': c,
        'positions': positions,
        'norm_attn_g': 1.0 + nrm(ks[3], (DEPTH, D_MODEL), 0.02),
        'norm_ffn_g': 1.0 + nrm(ks[4], (DEPTH, D_MODEL), 0.02),
        'w_ada': nrm(ks[5], (DEPTH, D_MODEL, 6 * D_MODEL), 0.5 * D_MODEL ** -0.5),
        'b_ada': nrm(ks[6], (DEPTH, 6 * D_MODEL), 0.02),
        'w_in': nrm(ks[7], (DEPTH, D_MODEL, N_IN), D_MODEL ** -0.5),
        'hgrn_lb_logits': nrm(ks[8], (DEPTH, A_KEY), 0.5),
        'hgrn_norm_g': 1.0 + nrm(ks[9], (DEPTH, A_WIDTH), 0.02),
        'attn_sinks': nrm(ks[10], (DEPTH, B_HEADS), 1.0),
        'w_branch_a': nrm(ks[11], (DEPTH, A_WIDTH, D_MODEL), A_WIDTH ** -0.5),
        'w_branch_b': nrm(ks[12], (DEPTH, B_WIDTH, D_MODEL), B_WIDTH ** -0.5),
        'w_branch_c': nrm(ks[13], (DEPTH, C_WIDTH, D_MODEL), C_WIDTH ** -0.5),
        'w_out': nrm(ks[14], (DEPTH, D_MODEL, D_MODEL), D_MODEL ** -0.5),
        'router_w': nrm(ks[15], (D_MODEL, N_EXPERTS), D_MODEL ** -0.5),
        'router_b': nrm(ks[16], (N_EXPERTS,), 0.01),
        'w_gate': nrm(ks[17], (DEPTH, N_EXPERTS, D_MODEL, D_FF_EXPERT), D_MODEL ** -0.5),
        'w_up': nrm(ks[18], (DEPTH, N_EXPERTS, D_MODEL, D_FF_EXPERT), D_MODEL ** -0.5),
        'w_down': nrm(ks[19], (DEPTH, N_EXPERTS, D_FF_EXPERT, D_MODEL), D_FF_EXPERT ** -0.5),
        'final_norm_g': 1.0 + nrm(ks[20], (D_MODEL,), 0.02),
    }

def reference(x, c, positions, norm_attn_g, norm_ffn_g, w_ada, b_ada, w_in, hgrn_lb_logits,
              hgrn_norm_g, attn_sinks, w_branch_a, w_branch_b, w_branch_c, w_out,
              router_w, router_b, w_gate, w_up, w_down, final_norm_g):
    lb_all = jnp.cumsum(jax.nn.softmax(hgrn_lb_logits.astype(F32), axis=0), axis=0)
    lb_all = lb_all - lb_all[0:1]
    cond = jax.nn.silu(c)
    for l in range(DEPTH):
        mod = cond @ w_ada[l] + b_ada[l]
        shift1, scale1, gate1, shift2, scale2, gate2 = jnp.split(mod[:, None, :], 6, axis=-1)
        h = rms_norm(x, norm_attn_g[l]) * (1.0 + scale1) + shift1
        x = x + gate1 * mixer_block(h, positions, w_in[l], lb_all[l], hgrn_norm_g[l], attn_sinks[l],
                                    w_branch_a[l], w_branch_b[l], w_branch_c[l], w_out[l])
        h = rms_norm(x, norm_ffn_g[l]) * (1.0 + scale2) + shift2
        x = x + gate2 * moe_ffn(h, router_w, router_b, w_gate[l], w_up[l], w_down[l])
    return rms_norm(x, final_norm_g)


_drawn_inputs = setup_inputs


def setup_inputs(seed=0):
    import zlib

    import numpy as np

    out = dict(_drawn_inputs(seed))
    spreads = {}
    factors = {'hgrn_lb_logits': 4.12, 'hgrn_norm_g': 4.058, 'attn_sinks': 8.0, 'final_norm_g': 2.948}
    for name, (base, spread) in spreads.items():
        noise = np.random.default_rng([zlib.crc32(name.encode()), seed]).standard_normal(out[name].shape)
        drawn = base * np.exp(spread * noise) if base else spread * noise
        out[name] = jnp.asarray(drawn.astype(out[name].dtype))
    for name, factor in factors.items():
        out[name] = (out[name] * factor).astype(out[name].dtype)
    return out
```

```python
from contextlib import ExitStack

import numpy as np
import concourse.bass as bass
from concourse import mybir

F32 = mybir.dt.float32
I32 = mybir.dt.int32
U8 = mybir.dt.uint8
ACT = mybir.ActivationFunctionType
ALU = mybir.AluOpType
AX_X = mybir.AxisListType.X

P = 128
D = 1024
KD = D // P
S = 256
TT = S // P
DEPTH = 2
CHUNK = 64
AH = 4
AW = AH * P
NH = 8
HD = 64
IH = 4
TOPK = 64
NE = 32
NG = 8
EG = NE // NG
FF = 256
FB = FF // P
CAP = 64
W_GATES = 3780
EPS = 1e-6
INADMISSIBLE = -3.0e38
CHOSEN = -3.4e38
MASKED = -1.0e30

HB_Q, HB_K, HC_Q, HC_K, HI_Q, HI_K, NHEADS = 0, 8, 12, 20, 22, 26, 28
NPAIR = NHEADS // 2
PB_Q, PB_K, PC_Q, PC_K, PI_Q, PI_K = (h // 2 for h in (HB_Q, HB_K, HC_Q, HC_K, HI_Q, HI_K))
LEVELS = [32, 16, 8, 4, 2, 1]

C_ID, C_ONE, C_UP, C_IOTA, C_B0, C_B1, C_KEEP, C_FREQ, C_GC, C_LC, C_PICK, C_EPS, NCONST = (
    0, 128, 256, 384, 512, 640, 896, 1152, 1184, 1192, 1224, 1225, 1226)

RING = 6
SLOT = 4096
GRANULES = ([f"ada{n}" for n in range(12)] + [f"in{n}" for n in range(8)]
            + ["gA0", "gA1", "wA", "gB0", "gB1", "wB", "gC0", "gC1", "wC", "out0", "out1"])
HOLES = (14, 17, 20, 25, 30)
PRE = 36
POS = [q for q in range(PRE) if q not in HOLES]
assert len(POS) == len(GRANULES) and PRE % RING == 0
NPRE = len(GRANULES)
MOE = 6 * NG
PRE_FILLS = [sum(q % RING == s for q in POS) for s in range(RING)]


def granule(name):
    n = GRANULES.index(name)
    q = POS[n]
    before = [GRANULES[m] for m in range(n) if POS[m] % RING == q % RING]
    return q % RING, len(before) + 1, before[-1] if before else None


def last_granule(slot):
    return [GRANULES[m] for m in range(NPRE) if POS[m] % RING == slot][-1]


GROUPS4 = [(hg, t) for t in range(TT) for hg in range(2)]


def attention_units(x):
    return [x + u for u in ("S0", "S1", "T0", "S2", "V0", "T1", "S3", "V1", "T2", "V2", "T3", "V3")]


UNITS = ([f"ada{n}" for n in range(12)] + ["norm1"] + [f"in{n}" for n in range(8)]
         + ["gA0", "gA1"] + [f"level{i}" for i in range(7)] + ["kdT", "U0", "U1", "U2", "O", "yaT"]
         + [f"feat{i}" for i in range(4)] + ["index0", "index1"]
         + ["brA0", "brA1", "gB0", "gB1"] + attention_units("B") + ["brB0", "brB1", "gC0", "gC1"]
         + attention_units("C") + ["brC0", "brC1", "out0", "out1", "norm2", "h2tok0", "h2tok1",
                                   "router", "places"])
PER_PAIR = [len(UNITS[p::4]) for p in range(4)]

TWO_PI_1 = 6.28125
TWO_PI_2 = float(np.float32(np.round((2 * np.pi - TWO_PI_1) * 2 ** 20) / 2 ** 20))
TWO_PI_3 = float(np.float32(2 * np.pi - TWO_PI_1 - TWO_PI_2))
ROUND = 12582912.0
PI_SAFE = 3.1415925

K_DVE = 110


def constants():
    c = np.zeros((P, NCONST), np.float32)
    r = np.arange(P)
    c[:, C_ID:C_ID + P] = np.eye(P)
    c[:, C_ONE:C_ONE + P] = 1.0
    c[:, C_UP:C_UP + P] = r[:, None] < r[None, :]
    c[:, C_IOTA:C_IOTA + P] = r[None, :] % CAP
    for t, at in ((0, C_B0), (1, C_B1)):
        keys = np.arange(P * (t + 1))[None, :] // CHUNK
        query = (P * t + r[:, None]) // CHUNK
        c[:, at:at + P * (t + 1)] = np.where((keys == query) | (keys == query - 1), 0.0, MASKED)
    c[:, C_KEEP:C_KEEP + S] = (np.arange(S) % CHUNK != 0)[None, :]
    c[:, C_FREQ:C_FREQ + 32] = np.float32(10000.0) ** (-np.arange(32, dtype=np.float32) * np.float32(2.0) / np.float32(HD))
    c[:, C_GC:C_GC + NG] = NG - np.arange(NG)
    c[:, C_LC:C_LC + NE] = EG - np.arange(NE) % EG
    c[::32, C_PICK] = 1.0
    c[:, C_EPS] = EPS
    m = np.zeros((P, 7, P), np.float32)
    s, t = r[:, None], r[None, :]
    for i, h in enumerate(LEVELS):
        m[:, i] = (s // (2 * h) == t // (2 * h)) & (s // h % 2 == 0) & (t // h % 2 == 1)
    m[:, 6] = s == t
    return c, m.reshape(P, 7 * P)


def trunk(nc, a, out):
    with ExitStack() as ctx:
        def sb(name, shape, dt=F32):
            return ctx.enter_context(nc.sbuf_tensor(name, shape, dt))

        events = {}

        def ev(name):
            if name not in events:
                events[name] = ctx.enter_context(nc.semaphore(name))
            return events[name]

        ring = sb("ring", [P, RING, SLOT])
        xT = sb("xT", [P, KD, S])
        hT = sb("hT", [P, KD, S])
        heads = sb("heads", [P, TT, NHEADS, HD])
        feat = sb("feat", [P, NPAIR, S])
        gate = sb("gate", [P, KD, S])
        qT = sb("qT", [P, AH, S])
        kT = sb("kT", [P, AH, S])
        bT = sb("bT", [P, AH, S])
        ex0 = sb("ex0", [P, 1024])
        ex1 = sb("ex1", [P, 1024])
        qk = sb("qk", [P, 1024])
        intra = sb("intra", [P, 8, P])
        vtok = sb("vtok", [P, TT, AW])
        sgtok = sb("sgtok", [P, TT, AW])
        state = sb("state", [P, 3, AH, P])
        consts = sb("consts", [P, NCONST])
        levelmask = sb("levelmask", [P, 7, P], U8)
        bv = sb("bv", [P, TT, 2, HD])
        cv = sb("cv", [P, TT, HD])
        iw = sb("iw", [P, TT, IH])
        cosT = sb("cosT", [P, TT, 32])
        sinT = sb("sinT", [P, TT, 32])
        posi = sb("posi", [P, TT], I32)
        posf = sb("posf", [P, TT])
        score0 = sb("score0", [P, P])
        score1 = sb("score1", [P, S])
        top8 = sb("top8", [P, 8])
        spare = sb("spare", [P, 1])
        pcol = sb("pcol", [P, 160])
        lb = sb("lb", [P, 2, 2, AH])
        lbtmp = sb("lbtmp", [P, 6, AH])
        cond32 = sb("cond32", [P, KD, 32])
        cond = sb("cond", [P, KD])
        mod = sb("mod", [P, 48])
        cur = sb("cur", [P, 16 + 48 + 2 * AH])
        gain1 = sb("gain1", [P, KD])
        gain2 = sb("gain2", [P, KD])
        dec = sb("dec", [P, 16])
        small = sb("small", [P, 8, 8])
        sinks = sb("sinks", [P, DEPTH * NH])
        sinkc = sb("sinkc", [P, NH])
        rw = sb("rw", [P, KD, NE])
        rb = sb("rb", [P, NE])
        aff = sb("aff", [P, TT, NE])
        rg = sb("rg", [P, 8, TT * NG])
        gsel = sb("gsel", [P, TT, NG])
        comb = sb("comb", [P, TT, NE])
        place = sb("place", [P, TT])
        passes = sb("passes", [P, 8])
        passi = sb("passi", [1, 4], I32)
        passf = sb("passf", [1, 4])
        wsel = sb("wsel", [P, NG, 2])

        ident = consts[:, C_ID:C_ID + P]
        ones = consts[:, C_ONE:C_ONE + P]
        upper = consts[:, C_UP:C_UP + P]
        iota = consts[:, C_IOTA:C_IOTA + P]

        def words(ap, n, at=0):
            nd = len(ap.shape)
            if nd == 3:
                flat = ap[:].rearrange("p a b -> p (a b)")
            elif nd == 4:
                flat = ap[:].rearrange("p a b c -> p (a b c)")
            else:
                flat = ap[:]
            return flat[:, at:at + n]

        squares = words(heads, KD * S).rearrange("p (k t) -> p k t", k=KD)
        merged = words(heads, KD * S).rearrange("p (k t) -> p k t", k=KD)
        xtok = words(feat, TT * D).rearrange("p (t d) -> p t d", t=TT)
        h2tok = xtok
        sin_x1 = words(feat, TT * NHEADS * 32).rearrange("p (t h d) -> p t h d", t=TT, h=NHEADS)
        sin_x2 = words(feat, TT * NHEADS * 32, TT * NHEADS * 32).rearrange("p (t h d) -> p t h d", t=TT, h=NHEADS)
        yaT, ybT, ycT = bT, qT, kT
        adarow = words(ex0, 1024).rearrange("p (r n) -> p r n", r=2)
        rt = words(ex0, 8 * TT * NE).rearrange("p (i n) -> p i n", i=8)
        one_hot = words(ex0, TT * P, 512).rearrange("p (t n) -> p t n", t=TT)
        var, rstd = words(ex1, S), words(ex1, S, S)
        ropetmp = words(ex1, 3 * TT * 32, 2 * S).rearrange("p (i t n) -> p i t n", i=3, t=TT)
        prow = words(ex1, 2 * P, 768).rearrange("p (i n) -> p i n", i=2)
        hgain = state[:, 2].rearrange("p h d -> p (h d)")
        att = [ex0[:], qk[:]]
        probT = [ex1[:], words(vtok, 1024)]
        slots1 = words(gate, TT * NG * P).rearrange("p (t g s) -> p t g s", t=TT, g=NG)
        slotsT = words(heads, NG * S).rearrange("p (g t) -> p g t", g=NG)
        hg = words(qT, KD * CAP).rearrange("p (k s) -> p k s", k=KD)
        silu_g = words(qT, 2 * FF, 512).rearrange("p (r f) -> p r f", r=2)
        he = words(kT, 2 * FF).rearrange("p (r f) -> p r f", r=2)
        heT = words(kT, 2 * FF, 512).rearrange("p (r f) -> p r f", r=2)
        yslot = words(bT, D)

        psum = [ctx.enter_context(nc.psum_tensor(f"pair{i}", [P, 1024], F32)) for i in range(4)]

        def unit(name):
            i = UNITS.index(name)
            return i % 4, i // 4

        def bank(name):
            return psum[unit(name)[0]]

        def filled(eng, l, name):
            p, n = unit(name)
            eng.wait_ge(ev(f"psum_full{p}"), l * PER_PAIR[p] + (n + 1))

        def taken(eng, l, name):
            p, n = unit(name)
            eng.wait_ge(ev(f"psum_taken{p}"), l * PER_PAIR[p] + (n + 2))

        def full_of(name):
            return ev(f"psum_full{unit(name)[0]}")

        def taken_of(name):
            return ev(f"psum_taken{unit(name)[0]}")

        PLACE = (0, 2, 1, 3)

        def score_halves(name, w):
            return bank(name)[:].rearrange("p (r n) -> p r n", r=2)[:, :, 0:2 * w]

        def slot3(name, k):
            return ring[:, granule(name)[0], :].rearrange("p (k n) -> p k n", k=k)

        def take_wait():
            nc.vector.memset(spare[:], 0.0)

        block = ctx.enter_context(nc.Block())

        @block.sync
        def _(sp):
            sp.sem_inc(ev("hidden_full"), 2)
            sp.sem_inc(ev("down_done"), 2)
            for p in range(4):
                sp.sem_inc(ev(f"psum_taken{p}"), 1)
            sp.sem_inc(ev("scatter_added"), 1)

            def fetch(slot, parts):
                for dst, src in parts:
                    sp.dma_start(dst, src).then_inc(ev(f"landed{slot}"), 16)

            def cols(w, l, lo, n, slot):
                src = w[bass.ds(l, 1), :, lo:lo + n].rearrange("o (k p) n -> p (o k) n", p=P)
                dst = ring[:, slot, 0:KD * n].rearrange("p (k n) -> p k n", k=KD)
                return [(dst[:, 4 * i:4 * i + 4, :], src[:, 4 * i:4 * i + 4, :]) for i in range(2)]

            def rows(w, l, slot):
                src = w[bass.ds(l, 1)].rearrange("o (k p) n -> p (o k) n", p=P)
                dst = ring[:, slot, :].rearrange("p (k n) -> p k n", k=4)
                return [(dst[:, 2 * i:2 * i + 2, :], src[:, 2 * i:2 * i + 2, :]) for i in range(2)]

            def expert_parts(l, g):
                for e in range(EG):
                    dst = ring[:, e, :].rearrange("p (k n) -> p k n", k=KD)
                    yield e, [(dst[:, :, u * FF:(u + 1) * FF],
                               a[w][bass.ds(l, 1), bass.ds(g * EG + e, 1)].rearrange("a b (k p) n -> p (a b k) n", p=P))
                              for u, w in enumerate(("w_gate", "w_up"))]
                for r in range(2):
                    dst = ring[:, EG + r, :].rearrange("p (e k n) -> p e k n", e=2, k=FB)
                    yield EG + r, [(dst[:, e], a["w_down"][bass.ds(l, 1), bass.ds(g * EG + 2 * r + e, 1)]
                                    .rearrange("a b (k p) n -> p (a b k) n", p=P)) for e in range(2)]

            def wait_expert_slot(slot, pair_count):
                name = "hidden_full" if slot < EG else "down_done"
                sp.wait_ge(ev(name), pair_count + (slot // 2 if slot < EG else slot - EG) + 1)

            def wait_reader(l, name):
                if name.startswith("ada"):
                    sp.wait_ge(ev("ada_rows"), l * 12 + (int(name[3:]) + 1))
                else:
                    filled(sp, l, f"br{name[1]}1" if name[0] == "w" else name)

            def fetch_experts(l, t, g):
                for slot, parts in expert_parts(l, g):
                    wait_expert_slot(slot, t * (2 * NG) + g * 2)
                    fetch(slot, parts)

            with sp.Fori(0, DEPTH) as l:
                sp.wait_ge(ev("pass_count"), l + 1)
                done = sp.value_load(passi[0:1, bass.ds(l, 1)], min_val=0, max_val=8)
                for name in GRANULES:
                    slot, _, before = granule(name)
                    if before is None:
                        wait_expert_slot(slot, done * (2 * NG))
                    else:
                        wait_reader(l, before)
                    if name.startswith("ada"):
                        fetch(slot, cols(a["w_ada"], l, 512 * int(name[3:]), 512, slot))
                    elif name.startswith("in"):
                        i = int(name[2:])
                        fetch(slot, cols(a["w_in"], l, 512 * i, min(512, W_GATES - 512 * i), slot))
                    elif name[0] == "g":
                        fetch(slot, cols(a["w_in"], l, W_GATES + D * "ABC".index(name[1]) + 512 * int(name[2]), 512, slot))
                    elif name[0] == "w":
                        fetch(slot, rows(a["w_branch_" + name[1].lower()], l, slot))
                    else:
                        fetch(slot, cols(a["w_out"], l, 512 * int(name[3:]), 512, slot))
                for slot, parts in expert_parts(l, 0):
                    wait_reader(l, last_granule(slot))
                    fetch(slot, parts)
                with sp.Fori(1, NG) as g:
                    fetch_experts(l, done, g)
                sp.wait_ge(ev("pass_count"), l + 2)
                end = sp.value_load(passi[0:1, bass.ds(l + 1, 1)], min_val=0, max_val=8)
                with sp.If(end > done + 1):
                    with sp.Fori(done + 1, end) as t:
                        with sp.Fori(0, NG) as g:
                            fetch_experts(l, t, g)
                sp.end_ifs()
            sp.wait_ge(ev("out_stored"), 32)

        @block.gpsimd
        def _(gp):
            n = [0]

            def load(dst, src, **how):
                gp.dma_start(dst, src, **how).then_inc(ev("small_loaded"), 16)
                n[0] += 1
            for t in range(TT):
                gp.dma_start(xtok[:, t, :], a["x"][0, P * t:P * t + P, :]).then_inc(ev("x_loaded"), 16)
            load(consts[:], a["constants"])
            load(qk[:, 0:7 * P], a["level_masks"])
            load(prow[0:8, 0, :], a["c"].rearrange("o (k p) -> (o k) p", p=P))
            load(prow[8:24, 0, :], a["norm_attn_g"].rearrange("o (k p) -> (o k) p", p=P))
            load(prow[24:40, 0, :], a["norm_ffn_g"].rearrange("o (k p) -> (o k) p", p=P))
            load(prow[40:48, 0, :], a["final_norm_g"].rearrange("(k p) -> k p", p=P))
            load(prow[48:56, 0, :], a["hgrn_lb_logits"].rearrange("o (k p) -> (o k) p", p=P))
            load(prow[0:96, 1, :], a["b_ada"].rearrange("o (k p) -> (o k) p", p=P))
            load(posi[:], a["positions"].rearrange("o (t p) -> p (o t)", p=P), allow_slow_non_contiguous=True)
            load(sinks[:], a["attn_sinks"].rearrange("l h -> (l h)").partition_broadcast(P))
            load(rb[:], a["router_b"].partition_broadcast(P))
            load(rw[:], a["router_w"].rearrange("(k p) n -> p k n", p=P))
            assert n[0] == NSMALL
            gp.memset(words(intra, 1024), 0.0).then_inc(ev("intra_zeroed"), 1)
            with gp.Fori(0, DEPTH) as l:
                gp.wait_ge(ev("pass_count"), l + 1)
                gp.dma_start(hgain, a["hgrn_norm_g"][bass.ds(l, 1), :].rearrange("o n -> (o n)").partition_broadcast(P)).then_inc(ev("hgain_loaded"), 16)

        @block.tensor
        def _(pe):
            mm = nc.tensor.matmul
            tr = nc.tensor.transpose
            order = [0]

            def claim(l, name):
                assert UNITS[order[0] % len(UNITS)] == name, (UNITS[order[0]], name)
                order[0] += 1
                p, n = unit(name)
                pe.wait_ge(ev(f"psum_taken{p}"), l * PER_PAIR[p] + (n + 1))
                return psum[p]

            def landed(l, done, name):
                slot, fills, _ = granule(name)
                pe.wait_ge(ev(f"landed{slot}"), l * (32 * PRE_FILLS[slot]) + done * (32 * NG) + 32 * fills)

            pe.wait_ge(ev("small_loaded"), 16 * NSMALL)
            pe.wait_ge(ev("x_loaded"), 16 * TT)
            for i in range(2):
                for k in range(4):
                    for t in range(TT):
                        m = tr(psum[i][:, k * S + t * P:k * S + t * P + P], xtok[:, t, (4 * i + k) * P:(4 * i + k + 1) * P], ident)
                m.then_inc(ev("x_turned"), 1)
            tr(psum[2][:, 0:56], prow[0:56, 0, :], ident[0:56, 0:56])
            tr(psum[2][:, 64:160], prow[0:96, 1, :], ident[0:96, 0:96]).then_inc(ev("params_turned"), 1)
            pe.wait_ge(ev("x_ready"), 2)
            pe.wait_ge(ev("params_ready"), 1)
            pe.wait_ge(ev("cond_ready"), 1)

            def norm_sum(dst, done_sem, sq_sem, base):
                for k in range(KD):
                    if k % 4 == 0:
                        pe.wait_ge(ev(sq_sem), base + (k // 4 + 1))
                    m = mm(dst[:, 0:S], ones, squares[:, k, :], start=k == 0, stop=k == KD - 1)
                m.then_inc(done_sem, 1)

            def cols_unit(l, name, rhs, kn):
                w = slot3(name, KD)
                dst = claim(l, name)
                for j in range(4):
                    for k in range(kn):
                        m = mm(dst[:, j * S:(j + 1) * S], w[:, k, j * P:(j + 1) * P], rhs[:, k, :], start=k == 0, stop=k == kn - 1)
                return m

            with pe.Fori(0, DEPTH) as l:
                pe.wait_ge(ev("pass_count"), l + 1)
                done = pe.value_load(passi[0:1, bass.ds(l, 1)], min_val=0, max_val=8)

                def ada_columns(n):
                    taken_row = ev("ada_row")
                    pe.wait_ge(taken_row, l * 12 + (n + 1))
                    dst = bank(f"ada{n}")
                    for j in range(4):
                        m = mm(dst[:, 512 + j:513 + j], adarow[:, n % 2, j * P:(j + 1) * P], consts[:, C_PICK:C_PICK + 1], start=True, stop=True)
                    m.then_inc(full_of(f"ada{n}"), 1)
                for n in range(12):
                    landed(l, done, f"ada{n}")
                    w = slot3(f"ada{n}", KD)
                    dst = claim(l, f"ada{n}")
                    for k in range(2):
                        for j in range(4):
                            m = mm(dst[32 * j:32 * j + 32, 0:512], cond32[:, 2 * j + k, :], w[:, 2 * j + k, :], start=k == 0, stop=k == 1)
                    m.then_inc(ev("ada_rows"), 1)
                    if n:
                        ada_columns(n - 1)
                ada_columns(11)

                norm_sum(claim(l, "norm1"), full_of("norm1"), "squared1", l * 2)

                pe.wait_ge(ev("h1_dve"), l + 1)
                pe.wait_ge(ev("h1_act"), l + 1)
                for i in range(8):
                    name = f"in{i}"
                    landed(l, done, name)
                    if i < 2:
                        m = cols_unit(l, name, hT, KD)
                    else:
                        n = min(512, W_GATES - 512 * i)
                        w = ring[:, granule(name)[0], 0:KD * n].rearrange("p (k n) -> p k n", k=KD)
                        dst = claim(l, name)
                        for t in range(TT):
                            for k in range(KD):
                                m = mm(dst[:, 512 * t:512 * t + n], hT[:, k, t * P:t * P + P], w[:, k, :], start=k == 0, stop=k == KD - 1)
                    m.then_inc(full_of(name), 1)

                def gates(x):
                    for i in range(2):
                        name = f"g{x}{i}"
                        landed(l, done, name)
                        cols_unit(l, name, hT, KD).then_inc(full_of(name), 1)
                gates("A")

                for i in range(7):
                    dst = claim(l, f"level{i}")
                    if i < 6:
                        pe.wait_ge(ev("level_scaled"), l * 6 + (i + 1))
                    for j in range(8):
                        lhs = words(kT, P, j * P) if i == 6 else qk[:, j * P:(j + 1) * P]
                        rhs = words(qT, P, j * P) if i == 6 else qk[:, j * P:(j + 1) * P]
                        m = mm(dst[:, j * P:(j + 1) * P], lhs, rhs, start=True, stop=True)
                    m.then_inc(full_of(f"level{i}"), 1)
                dst = claim(l, "kdT")
                pe.wait_ge(ev("kd_ready"), l + 1)
                for j in range(8):
                    m = tr(dst[:, j * P:(j + 1) * P], qk[:, j * P:(j + 1) * P], ident)
                m.then_inc(full_of("kdT"), 1)
                taken(pe, l, "kdT")
                taken(pe, l, "in2")
                for c in range(3):
                    dst = claim(l, f"U{c}")
                    r = CHUNK * (c % 2)
                    for h in range(AH):
                        at = (2 * h + c // 2) * P
                        m = mm(dst[:, h * P:(h + 1) * P], ex1[r:r + CHUNK, at:at + P], vtok[r:r + CHUNK, c // 2, h * P:(h + 1) * P], start=True, stop=True)
                    m.then_inc(full_of(f"U{c}"), 1)
                dst = claim(l, "O")
                taken(pe, l, "level6")
                pe.wait_ge(ev("qe_ready"), l + 1)
                taken(pe, l, "U2")
                for t in range(TT):
                    for h in range(AH):
                        o = 512 * t + h * P
                        m = mm(dst[:, o:o + P], intra[:, 2 * h + t, :], vtok[:, t, h * P:(h + 1) * P], start=True, stop=False, skip_group_check=True)
                        for c in ((1,) if t == 0 else (2, 3)):
                            r = CHUNK * (c % 2)
                            m = mm(dst[r:r + CHUNK, o:o + P], qT[:, h, c * CHUNK:(c + 1) * CHUNK], state[:, c - 1, h, :], start=False, stop=True, skip_group_check=True)
                m.then_inc(full_of("O"), 1)
                dst = claim(l, "yaT")
                pe.wait_ge(ev("ya_ready"), l + 1)
                for t in range(TT):
                    for h in range(AH):
                        m = tr(dst[:, h * S + t * P:h * S + t * P + P], qk[:, 512 * t + h * P:512 * t + h * P + P], ident)
                m.then_inc(full_of("yaT"), 1)

                for i in range(4):
                    dst = claim(l, f"feat{i}")
                    if i == 0:
                        pe.wait_ge(ev("roped"), l + 1)
                    for p in range(4 * i, min(4 * i + 4, NPAIR)):
                        for t in range(TT):
                            src = heads[:, t, 2 * p:2 * p + 2, :].rearrange("p h d -> p (h d)")
                            m = tr(dst[:, (p % 4) * S + t * P:(p % 4) * S + t * P + P], src, ident)
                    m.then_inc(full_of(f"feat{i}"), 1)
                for i in range(4):
                    taken(pe, l, f"feat{i}")
                for t in range(TT):
                    w = P * (t + 1)
                    dst = claim(l, f"index{t}")
                    for h in range(IH):
                        r = HD * (h % 2)
                        at = 512 * (h % 2) + (h // 2) * w
                        m = mm(dst[:, at:at + w], feat[r:r + HD, PI_Q + h // 2, t * P:t * P + P], feat[r:r + HD, PI_K, 0:w], start=True, stop=True)
                    m.then_inc(full_of(f"index{t}"), 1)

                def branch(x, y):
                    landed(l, done, f"w{x}")
                    w = slot3(f"w{x}", 4)
                    for i in range(2):
                        dst = claim(l, f"br{x}{i}")
                        for j in range(4):
                            for k in range(4):
                                m = mm(dst[:, j * S:(j + 1) * S], w[:, k, (4 * i + j) * P:(4 * i + j + 1) * P], y[:, k, :], start=k == 0, stop=k == 3)
                        m.then_inc(full_of(f"br{x}{i}"), 1)

                taken(pe, l, "yaT")
                branch("A", yaT)
                gates("B")

                def attention(x, qp, kp, values):
                    def scores(i):
                        hg_, t = GROUPS4[i]
                        w = P * (t + 1)
                        dst = claim(l, f"{x}S{i}")
                        for j in range(4):
                            h = 4 * hg_ + j
                            r = HD * (h % 2)
                            at = 512 * (j % 2) + (j // 2) * w
                            m = mm(dst[:, at:at + w], feat[r:r + HD, qp + h // 2, t * P:t * P + P], feat[r:r + HD, kp(h), 0:w], start=True, stop=True)
                        m.then_inc(full_of(f"{x}S{i}"), 1)

                    def turn(i):
                        _, t = GROUPS4[i]
                        dst = claim(l, f"{x}T{i}")
                        pe.wait_ge(ev(f"probs_{x}"), l * 4 + (i + 1))
                        for j in range(4 * (t + 1)):
                            m = tr(dst[:, j * P:(j + 1) * P], att[i % 2][:, j * P:(j + 1) * P], ident)
                        m.then_inc(full_of(f"{x}T{i}"), 1)

                    def weigh(i):
                        _, t = GROUPS4[i]
                        dst = claim(l, f"{x}V{i}")
                        taken(pe, l, f"{x}T{i}")
                        for j in range(4):
                            r = HD * (j % 2)
                            for kt in range(t + 1):
                                m = mm(dst[r:r + HD, (j // 2) * P:(j // 2 + 1) * P], values(4 * GROUPS4[i][0] + j, kt),
                                       probT[i % 2][:, (PLACE[j] * (t + 1) + kt) * P:(PLACE[j] * (t + 1) + kt + 1) * P], start=kt == 0, stop=kt == t)
                        m.then_inc(full_of(f"{x}V{i}"), 1)
                    scores(0); scores(1)
                    turn(0); scores(2); weigh(0)
                    turn(1); scores(3); weigh(1)
                    turn(2); weigh(2); turn(3); weigh(3)
                    taken(pe, l, f"{x}V2")
                    taken(pe, l, f"{x}V3")

                attention("B", PB_Q, lambda h: PB_K + h // 4, lambda h, kt: bv[:, kt, h // 4, :])
                branch("B", ybT)
                gates("C")
                attention("C", PC_Q, lambda h: PC_K, lambda h, kt: cv[:, kt, :])
                branch("C", ycT)

                pe.wait_ge(ev("merged"), l + 1)
                for i in range(2):
                    landed(l, done, f"out{i}")
                    cols_unit(l, f"out{i}", merged, KD).then_inc(full_of(f"out{i}"), 1)

                norm_sum(claim(l, "norm2"), full_of("norm2"), "squared2", l * 2)
                pe.wait_ge(ev("h2_dve"), l + 1)
                pe.wait_ge(ev("h2_act"), l + 1)
                for t in range(TT):
                    dst = claim(l, f"h2tok{t}")
                    for k in range(KD):
                        m = tr(dst[:, k * P:(k + 1) * P], hT[:, k, t * P:t * P + P], ident)
                    m.then_inc(full_of(f"h2tok{t}"), 1)
                dst = claim(l, "router")
                for t in range(TT):
                    for k in range(KD):
                        m = mm(dst[:, t * NE:(t + 1) * NE], hT[:, k, t * P:t * P + P], rw[:, k, :], start=k == 0, stop=k == KD - 1)
                m.then_inc(full_of("router"), 1)
                dst = claim(l, "places")
                pe.wait_ge(ev("group_chosen"), l + 1)
                mm(dst[:, 0:NG], upper, gsel[:, 0, :], start=True, stop=True)
                mm(dst[:, NG:2 * NG], ones, gsel[:, 0, :], start=True, stop=False)
                mm(dst[:, NG:2 * NG], upper, gsel[:, 1, :], start=False, stop=True)
                mm(dst[:, 2 * NG:3 * NG], ones, gsel[:, 0, :], start=True, stop=False)
                mm(dst[:, 2 * NG:3 * NG], ones, gsel[:, 1, :], start=False, stop=True).then_inc(full_of("places"), 1)

                for p in range(4):
                    pe.wait_ge(ev(f"psum_taken{p}"), l * PER_PAIR[p] + (PER_PAIR[p] + 1))
                pe.wait_ge(ev("pass_count"), l + 2)
                end = pe.value_load(passi[0:1, bass.ds(l + 1, 1)], min_val=0, max_val=8)
                with pe.Fori(done, end) as t_:
                    pe.wait_ge(ev("slots_ready"), t_ + 1)
                    for i in range(2):
                        for g in range(4):
                            for t in range(TT):
                                m = tr(psum[i][:, g * S + t * P:g * S + t * P + P], slots1[:, t, 4 * i + g, :], ident)
                        m.then_inc(ev("slots_turned"), 1)
                    for g in range(NG):
                        for t in range(TT):
                            m = mm(psum[2][:, EG * g:EG * g + EG], slots1[:, t, g, :], comb[:, t, EG * g:EG * g + EG], start=t == 0, stop=t == TT - 1)
                    m.then_inc(ev("slot_weights"), 1)
                    with pe.Fori(0, NG) as g:
                        pe.wait_ge(ev("slotsT_ready"), t_ * 2 + 2)
                        pe.wait_ge(ev("wsel_ready"), t_ * 2 + 2)
                        for k in range(KD):
                            for t in range(TT):
                                m = mm(psum[0][:, k * CAP:(k + 1) * CAP], h2tok[:, t, k * P:(k + 1) * P],
                                       slots1[:, t, bass.ds(g, 1), 0:CAP].rearrange("p o s -> p (o s)"), start=t == 0, stop=t == TT - 1)
                        m.then_inc(ev("gathered"), 1)
                        pe.wait_ge(ev("hg_ready"), t_ * NG + g + 1)

                        def arrived(slot):
                            pe.wait_ge(ev(f"landed{slot}"), l * (32 * PRE_FILLS[slot]) + t_ * (32 * NG) + g * 32 + (32 * PRE_FILLS[slot] + 32))

                        for r in range(2):
                            arrived(2 * r)
                            arrived(2 * r + 1)
                            for k in range(KD):
                                for j in range(2):
                                    w = ring[:, 2 * r + j, :].rearrange("p (k n) -> p k n", k=KD)
                                    m = mm(psum[1][CAP * j:CAP * j + CAP, 512 * r:512 * r + 512], hg[:, k, :], w[:, k, :], start=k == 0, stop=k == KD - 1)
                            m.then_inc(ev("hidden_full"), 1)
                        for r in range(2):
                            pe.wait_ge(ev("he_ready"), t_ * (2 * NG) + g * 2 + (r + 1))
                            for f in range(FB):
                                m = tr(psum[0][:, 512 + f * P:512 + (f + 1) * P], he[:, r, f * P:(f + 1) * P], ident)
                            m.then_inc(ev("he_turned"), 1)
                            pe.wait_ge(ev("heT_ready"), t_ * (2 * NG) + g * 2 + (r + 1))
                            arrived(EG + r)
                            w = ring[:, EG + r, :].rearrange("p (e k n) -> p e k n", e=2, k=FB)
                            for f in range(FB):
                                for half in range(2):
                                    for j in range(2):
                                        m = mm(psum[2][CAP * j:CAP * j + CAP, 512 * half:512 * half + 512], heT[:, r, f * P + CAP * j:f * P + CAP * j + CAP],
                                               w[:, j, f, 512 * half:512 * half + 512], start=(r == 0 and f == 0), stop=(r == 1 and f == FB - 1))
                            m.then_inc(ev("down_done"), 1)
                        pe.wait_ge(ev("yslot_ready"), t_ * NG + g + 1)
                        for i in range(2):
                            pe.wait_ge(ev("scatter_added"), t_ * (2 * NG) + g * 2 + (i + 1))
                            for j in range(4):
                                m = mm(psum[3][:, j * S:(j + 1) * S], yslot[:, (4 * i + j) * P:(4 * i + j + 1) * P],
                                       slotsT[:, bass.ds(g, 1), :].rearrange("p o t -> p (o t)"), start=True, stop=True)
                            m.then_inc(ev("scattered"), 1)
                pe.wait_ge(ev("scatter_added"), end * (2 * NG) + 1)

            norm_sum(psum[0], ev("final_sum"), "squared3", 0)
            pe.wait_ge(ev("final_ready"), 1)
            for t in range(TT):
                for k in range(KD):
                    m = tr(psum[1 + t][:, k * P:(k + 1) * P], hT[:, k, t * P:t * P + P], ident)
                m.then_inc(ev("final_turned"), 1)

        @block.scalar
        def _(ac):
            act = nc.scalar.activation
            ac.wait_ge(ev("params_ready"), 1)
            act(cond[:], pcol[:, 0:KD], ACT.Silu).then_inc(ev("cond_silu"), 1)
            ac.wait_ge(ev("lb_shifted"), 1)
            act(lbtmp[:, 3:5, :], lbtmp[:, 1:3, :], ACT.Exp).then_inc(ev("lb_exp"), 1)
            ac.wait_ge(ev("angles"), 1)
            act(sinT[:], ropetmp[:, 1], ACT.Sin).then_inc(ev("rope_table"), 1)
            ac.wait_ge(ev("angles"), 2)
            act(cosT[:], ropetmp[:, 2], ACT.Sin).then_inc(ev("rope_table"), 1)
            ac.wait_ge(ev("x_ready"), 2)

            def squares_of_x(name):
                for i in range(2):
                    act(squares[:, 4 * i:4 * i + 4, :], xT[:, 4 * i:4 * i + 4, :], ACT.Square).then_inc(ev(name), 1)

            with ac.Fori(0, DEPTH) as l:
                ac.wait_ge(ev("pass_count"), l + 1)
                done = ac.value_load(passi[0:1, bass.ds(l, 1)], min_val=0, max_val=8)
                ac.wait_ge(ev("scatter_added"), done * (2 * NG) + 1)
                squares_of_x("squared1")
                for n in range(12):
                    p, _ = unit(f"ada{n}")
                    ac.wait_ge(ev("ada_rows"), l * 12 + (n + 1))
                    if n >= 2:
                        filled(ac, l, f"ada{n - 2}")
                    act(adarow[:, n % 2, :], psum[p][:, 0:512], ACT.Copy).then_inc(ev("ada_row"), 1)

                def root(src, dst, ready, name, l1):
                    ac.wait_ge(ev(ready), l1)
                    act(dst, src, ACT.Sqrt).then_inc(ev(name), 1)

                def modulate(which, l1, shift, gain):
                    ac.wait_ge(ev(f"h{which}_scaled"), l1)
                    for k in range(4, KD):
                        ins = act(hT[:, k, :], hT[:, k, :], ACT.Identity, bias=mod[:, shift + k:shift + k + 1], scale=gain[:, k:k + 1])
                    ins.then_inc(ev(f"h{which}_act"), 1)
                root(var[:], rstd[:], "var1", "root1", l + 1)
                modulate(1, l + 1, 0, gain1)

                filled(ac, l, "in0")
                act(words(qT, 1024), bank("in0")[:], ACT.Silu).then_inc(taken_of("in0"), 1)
                filled(ac, l, "in1")
                act(ex0[:], bank("in1")[:], ACT.Sigmoid).then_inc(taken_of("in1"), 1)
                filled(ac, l, "in2")
                act(words(vtok, 1024), bank("in2")[:], ACT.Copy).then_inc(taken_of("in2"), 1)
                filled(ac, l, "in3")
                act(words(sgtok, 1024), bank("in3")[:], ACT.Silu).then_inc(taken_of("in3"), 1)

                def by_token(name, lo, n):
                    return bank(name)[:].rearrange("p (t n) -> p t n", t=TT)[:, :, lo:lo + n]

                def to_heads(name, lo, h, n, step=1):
                    src = by_token(name, lo, n * HD).rearrange("p t (h d) -> p t h d", h=n)
                    return act(heads[:, :, h:h + (n - 1) * step + 1:step, :], src, ACT.Copy)
                filled(ac, l, "in4")
                to_heads("in4", 0, HB_Q, 8).then_inc(taken_of("in4"), 1)
                filled(ac, l, "in5")
                to_heads("in5", 0, HB_K, 2, 2)
                to_heads("in5", 0, HB_K + 1, 2, 2)
                act(bv[:].rearrange("p t h d -> p t (h d)"), by_token("in5", 128, 128), ACT.Copy)
                to_heads("in5", 256, HC_Q, 4).then_inc(taken_of("in5"), 1)
                filled(ac, l, "in6")
                to_heads("in6", 0, HC_Q + 4, 4)
                to_heads("in6", 256, HC_K, 1)
                to_heads("in6", 256, HC_K + 1, 1)
                act(cv[:], by_token("in6", 320, HD), ACT.Copy)
                to_heads("in6", 384, HI_Q, 2).then_inc(taken_of("in6"), 1)
                filled(ac, l, "in7")
                to_heads("in7", 0, HI_Q + 2, 2)
                to_heads("in7", 128, HI_K, 1)
                to_heads("in7", 128, HI_K + 1, 1)
                act(iw[:], by_token("in7", 192, IH), ACT.Copy).then_inc(taken_of("in7"), 1)

                ac.wait_ge(ev("f_ready"), l + 1)
                act(qk[:], ex0[:], ACT.Ln).then_inc(ev("logf"), 1)

                def gates(x):
                    for i in range(2):
                        filled(ac, l, f"g{x}{i}")
                        if x == "B":
                            taken(ac, l, f"brA{i}")
                        if x == "C":
                            ac.wait_ge(ev("merged_B"), l * 2 + (i + 1))
                        act(gate[:, 4 * i:4 * i + 4, :].rearrange("p k t -> p (k t)"), bank(f"g{x}{i}")[:], ACT.Sigmoid).then_inc(taken_of(f"g{x}{i}"), 1)
                gates("A")

                for i, h in enumerate(LEVELS):
                    ex = (ex0, ex1)[i % 2]
                    ac.wait_ge(ev("level_diff"), l * 7 + (i + 1))
                    v = ex[:].rearrange("p (n w) -> p n w", w=2 * h)
                    act(v[:, :, 0:h], v[:, :, 0:h], ACT.Exp, scale=-1.0)
                    act(v[:, :, h:2 * h], v[:, :, h:2 * h], ACT.Exp).then_inc(ev("level_exp"), 1)
                ac.wait_ge(ev("level_scaled"), l * 6 + 5)
                act(ex0[:], words(bT, 1024), ACT.Exp).then_inc(ev("level_exp"), 1)
                act(dec[:], words(bT, 1024).rearrange("p (n w) -> p n w", w=CHUNK)[:, :, CHUNK - 1], ACT.Exp).then_inc(ev("decay"), 1)
                ac.wait_ge(ev("level_diff"), l * 7 + 7)
                act(ex1[:], ex1[:], ACT.Exp, scale=-1.0).then_inc(ev("level_exp"), 1)
                filled(ac, l, "kdT")
                act(ex1[:], bank("kdT")[:], ACT.Copy).then_inc(taken_of("kdT"), 1)
                filled(ac, l, "O")
                ac.wait_ge(ev("qe_ready"), l + 1)
                act(ex0[:], bank("O")[:], ACT.Square).then_inc(ev("o_squared"), 1)
                ac.wait_ge(ev("o_var"), l + 1)
                act(small[:, 1, :], small[:, 0, :], ACT.Sqrt).then_inc(ev("o_root"), 1)
                filled(ac, l, "yaT")
                act(words(yaT, 1024), bank("yaT")[:], ACT.Copy).then_inc(taken_of("yaT"), 1)

                for i in range(4):
                    n = min(4, NPAIR - 4 * i) * S
                    filled(ac, l, f"feat{i}")
                    act(words(feat, n, 1024 * i), bank(f"feat{i}")[:, 0:n], ACT.Copy).then_inc(taken_of(f"feat{i}"), 1)
                for t in range(TT):
                    filled(ac, l, f"index{t}")
                    if t:
                        ac.wait_ge(ev("score_summed"), l * 2 + 1)
                    w = P * (t + 1)
                    act(ex0[:, 0:4 * w].rearrange("p (r n) -> p r n", r=2), score_halves(f"index{t}", w), ACT.Relu).then_inc(taken_of(f"index{t}"), 1)

                gates("B")

                def attention(x, yT):
                    def exps(i):
                        hg_, t = GROUPS4[i]
                        w = P * (t + 1)
                        ac.wait_ge(ev(f"max_{x}"), l * 4 + (i + 1))
                        for j in range(4):
                            ins = act(att[i % 2][:, j * w:(j + 1) * w], att[i % 2][:, j * w:(j + 1) * w], ACT.Exp,
                                      bias=small[:, 2 + i % 2, j:j + 1], accum_out=small[:, 4 + i % 2, j:j + 1])
                        if x == "B":
                            ins = act(small[:, 6 + i % 2, 4:8], small[:, 6 + i % 2, 0:4], ACT.Exp)
                        ins.then_inc(ev(f"exp_{x}"), 1)

                    def out_of(kind, i):
                        hg_, t = GROUPS4[i]
                        name = f"{x}{kind}{i}"
                        filled(ac, l, name)
                        if kind == "T":
                            n = 512 * (t + 1)
                            act(probT[i % 2][:, 0:n], bank(name)[:, 0:n], ACT.Copy).then_inc(taken_of(name), 1)
                        else:
                            act(yT[:, 2 * hg_:2 * hg_ + 2, t * P:t * P + P], bank(name)[:, 0:2 * P].rearrange("p (k t) -> p k t", k=2),
                                ACT.Copy).then_inc(taken_of(name), 1)
                    exps(0); exps(1)
                    out_of("T", 0); exps(2); out_of("V", 0)
                    out_of("T", 1); exps(3); out_of("V", 1)
                    out_of("T", 2); out_of("V", 2); out_of("T", 3); out_of("V", 3)

                attention("B", ybT)
                gates("C")
                attention("C", ycT)

                taken(ac, l, "out1")
                squares_of_x("squared2")
                root(var[:], rstd[:], "var2", "root2", l + 1)
                modulate(2, l + 1, 24, gain2)
                for t in range(TT):
                    filled(ac, l, f"h2tok{t}")
                    act(h2tok[:, t, :], bank(f"h2tok{t}")[:], ACT.Copy).then_inc(taken_of(f"h2tok{t}"), 1)
                filled(ac, l, "router")
                act(words(aff, TT * NE), bank("router")[:, 0:TT * NE], ACT.Sigmoid).then_inc(taken_of("router"), 1)

                ac.wait_ge(ev("pass_count"), l + 2)
                end = ac.value_load(passi[0:1, bass.ds(l + 1, 1)], min_val=0, max_val=8)
                with ac.Fori(done, end) as t_:
                    for i in range(2):
                        ac.wait_ge(ev("slots_turned"), t_ * 2 + (i + 1))
                        act(slotsT[:, 4 * i:4 * i + 4, :].rearrange("p g t -> p (g t)"), psum[i][:], ACT.Copy).then_inc(ev("slotsT_ready"), 1)
                    with ac.Fori(0, NG) as g:
                        for r in range(2):
                            ac.wait_ge(ev("hidden_full"), t_ * (2 * NG) + g * 2 + (r + 3))
                            act(silu_g[:, r, :], psum[1][:, 512 * r:512 * r + FF], ACT.Silu).then_inc(ev("silu_ready"), 1)
                        for r in range(2):
                            ac.wait_ge(ev("he_turned"), t_ * (2 * NG) + g * 2 + (r + 1))
                            act(heT[:, r, :], psum[0][:, 512:512 + FF], ACT.Copy).then_inc(ev("heT_ready"), 1)
                        ac.wait_ge(ev("down_done"), t_ * (2 * NG) + g * 2 + 4)
                        act(yslot[:], psum[2][:], ACT.Copy).then_inc(ev("yslot_ready"), 1)

            done = ac.value_load(passi[0:1, DEPTH:DEPTH + 1], min_val=0, max_val=8)
            ac.wait_ge(ev("scatter_added"), done * (2 * NG) + 1)
            squares_of_x("squared3")
            root(var[:], rstd[:], "var3", "root3", 1)
            for t in range(TT):
                ac.wait_ge(ev("final_turned"), t + 1)
                act(h2tok[:, t, :], psum[1 + t][:], ACT.Copy).then_inc(ev("final_copied"), 1)
                ac.wait_ge(ev("final_copied"), t + 1)
                ac.dma_start(out[0, P * t:P * t + P, :], h2tok[:, t, :]).then_inc(ev("out_stored"), 16)

        @block.vector
        def _(dv):
            V = nc.vector
            chain = [0]

            def link(ins, l=0, alone=False):
                chain[0] += 1
                ins.then_inc(ev("dve_chain"), 1)
                dv.wait_ge(ev("dve_chain"), l * K_DVE + chain[0])
                if alone:
                    take_wait()

            link(V.memset(passi[:], 0))
            V.memset(passf[:], 0.0).then_inc(ev("pass_count"), 1)
            for i in range(2):
                dv.wait_ge(ev("x_turned"), i + 1)
                V.tensor_copy(xT[:, 4 * i:4 * i + 4, :].rearrange("p k t -> p (k t)"), psum[i][:]).then_inc(ev("x_ready"), 1)
            dv.wait_ge(ev("params_turned"), 1)
            link(V.tensor_copy(pcol[:, 0:56], psum[2][:, 0:56]))
            V.tensor_copy(pcol[:, 64:160], psum[2][:, 64:160]).then_inc(ev("params_ready"), 1)
            dv.wait_ge(ev("params_ready"), 1)
            z0, z1 = pcol[:, 48:52], pcol[:, 52:56]
            link(V.tensor_tensor(lbtmp[:, 0, :], z0, z1, ALU.max))
            link(V.tensor_tensor(lbtmp[:, 1, :], z0, lbtmp[:, 0, :], ALU.subtract))
            V.tensor_tensor(lbtmp[:, 2, :], z1, lbtmp[:, 0, :], ALU.subtract).then_inc(ev("lb_shifted"), 1)
            V.tensor_copy(words(levelmask, 7 * P), qk[:, 0:7 * P])
            link(V.tensor_copy(posf[:], posi[:]))
            for t in range(TT):
                link(V.tensor_scalar(ropetmp[:, 0, t, :], consts[:, C_FREQ:C_FREQ + 32], posf[:, t:t + 1], None, ALU.mult))
            for i, (turn, back) in enumerate(((0.0, 0.0), (0.25, np.pi / 2))):
                r, n = ropetmp[:, 1 + i], (sinT, cosT)[i]
                link(V.tensor_scalar(n[:], ropetmp[:, 0], 1.0 / (2 * np.pi), turn, ALU.mult, ALU.add))
                link(V.tensor_scalar(n[:], n[:], ROUND, None, ALU.add))
                link(V.tensor_scalar(n[:], n[:], -ROUND, None, ALU.add))
                link(V.scalar_tensor_tensor(out=r, in0=n[:], scalar=-TWO_PI_1, in1=ropetmp[:, 0], op0=ALU.mult, op1=ALU.add))
                link(V.scalar_tensor_tensor(out=r, in0=n[:], scalar=-TWO_PI_2, in1=r, op0=ALU.mult, op1=ALU.add))
                link(V.scalar_tensor_tensor(out=r, in0=n[:], scalar=-TWO_PI_3, in1=r, op0=ALU.mult, op1=ALU.add))
                link(V.tensor_scalar(r, r, float(back), PI_SAFE, ALU.add, ALU.min))
                V.tensor_scalar(r, r, -PI_SAFE, None, ALU.max).then_inc(ev("angles"), 1)
            dv.wait_ge(ev("cond_silu"), 1)
            V.tensor_copy(cond32[:], cond[:].unsqueeze(2).broadcast_to([P, KD, 32])).then_inc(ev("cond_ready"), 1)
            dv.wait_ge(ev("lb_exp"), 1)
            link(V.tensor_tensor(lbtmp[:, 0, :], lbtmp[:, 3, :], lbtmp[:, 4, :], ALU.add))
            link(V.reciprocal(lbtmp[:, 5, :], lbtmp[:, 0, :]))
            link(V.tensor_tensor(lbtmp[:, 3, :], lbtmp[:, 3, :], lbtmp[:, 5, :], ALU.mult))
            link(V.tensor_tensor(lbtmp[:, 4, :], lbtmp[:, 4, :], lbtmp[:, 5, :], ALU.mult))
            link(V.tensor_tensor(lbtmp[:, 4, :], lbtmp[:, 3, :], lbtmp[:, 4, :], ALU.add))
            link(V.tensor_tensor(lb[:, 0, 0, :], lbtmp[:, 3, :], lbtmp[:, 3, :], ALU.subtract))
            link(V.tensor_tensor(lb[:, 1, 0, :], lbtmp[:, 4, :], lbtmp[:, 3, :], ALU.subtract))
            for i in range(2):
                link(V.tensor_scalar(lb[:, i, 1, :], lb[:, i, 0, :], -1.0, 1.0, ALU.mult, ALU.add))
            link(V.memset(small[:], 0.0))
            first = chain[0]
            dv.wait_ge(ev("intra_zeroed"), 1)
            dv.wait_ge(ev("rope_table"), 2)

            with dv.Fori(0, DEPTH) as l:
                V.tensor_copy(cur[:, 0:8], pcol[:, bass.ds(l * 8 + 8, 8)])
                V.tensor_copy(cur[:, 8:16], pcol[:, bass.ds(l * 8 + 24, 8)])
                V.tensor_copy(cur[:, 16:64], pcol[:, bass.ds(l * 48 + 64, 48)])
                V.tensor_copy(sinkc[:], sinks[:, bass.ds(l * NH, NH)])
                link(V.tensor_copy(cur[:, 64:72], lb[:, bass.ds(l, 1)].rearrange("p o a h -> p (o a h)")), l)
                lbc, omc = cur[:, 64:68], cur[:, 68:72]
                for n in range(12):
                    p, _ = unit(f"ada{n}")
                    filled(dv, l, f"ada{n}")
                    V.tensor_tensor(mod[:, 4 * n:4 * n + 4], psum[p][:, 512:516], cur[:, 16 + 4 * n:20 + 4 * n], ALU.add).then_inc(ev(f"psum_taken{p}"), 1)
                taken(dv, l, "ada11")
                taken(dv, l, "ada10")
                taken(dv, l, "ada9")
                taken(dv, l, "ada8")
                V.scalar_tensor_tensor(out=gain1[:], in0=mod[:, 8:16], scalar=1.0, in1=cur[:, 0:8], op0=ALU.add, op1=ALU.mult)
                link(V.scalar_tensor_tensor(out=gain2[:], in0=mod[:, 32:40], scalar=1.0, in1=cur[:, 8:16], op0=ALU.add, op1=ALU.mult), l)

                def norm_unit(which, name, gain, shift):
                    filled(dv, l, name)
                    V.tensor_scalar(var[:], bank(name)[:, 0:S], 1.0 / D, EPS, ALU.mult, ALU.add).then_inc(ev(f"var{which}"), 1)
                    dv.wait_ge(ev(f"root{which}"), l + 1)
                    link(V.reciprocal(var[:], rstd[:]), l)
                    V.tensor_tensor(hT[:, 4:8, :], xT[:, 4:8, :], var[:].unsqueeze(1).broadcast_to([P, 4, S]), ALU.mult).then_inc(ev(f"h{which}_scaled"), 1)
                    V.tensor_tensor(hT[:, 0:4, :], xT[:, 0:4, :], var[:].unsqueeze(1).broadcast_to([P, 4, S]), ALU.mult).then_inc(taken_of(name), 1)
                    taken(dv, l, name)
                    for k in range(4):
                        ins = V.tensor_scalar(hT[:, k, :], hT[:, k, :], gain[:, k:k + 1], mod[:, shift + k:shift + k + 1], ALU.mult, ALU.add)
                    ins.then_inc(ev(f"h{which}_dve"), 1)
                norm_unit(1, "norm1", gain1, 0)

                taken(dv, l, "in1")
                f = ex0[:].rearrange("p (h t) -> p h t", h=AH)
                for h in range(AH):
                    ins = V.tensor_scalar(f[:, h, :], f[:, h, :], omc[:, h:h + 1], lbc[:, h:h + 1], ALU.mult, ALU.add)
                    if h == AH - 1:
                        link(ins, l)
                    else:
                        ins
                link(V.tensor_scalar(words(kT, 1024), ex0[:], -1.0, 1.0, ALU.mult, ALU.add), l)
                V.tensor_scalar(ex0[:], ex0[:], 2.0 ** -64, None, ALU.max).then_inc(ev("f_ready"), 1)
                dv.wait_ge(ev("logf"), l + 1)
                for h in range(AH):
                    ins = V.tensor_tensor_scan(bT[:, h, :], consts[:, C_KEEP:C_KEEP + S], qk[:, h * S:(h + 1) * S], 0.0, ALU.mult, ALU.add)
                link(ins, l)

                def diff(i):
                    h = LEVELS[i]
                    v = words(bT, 1024).rearrange("p (n w) -> p n w", w=2 * h)
                    ex = (ex0, ex1)[i % 2][:].rearrange("p (n w) -> p n w", w=2 * h)
                    V.tensor_tensor(ex, v, v[:, :, h - 1:h].broadcast_to([P, 512 // h, 2 * h]), ALU.subtract).then_inc(ev("level_diff"), 1)

                def scaled(i):
                    h = LEVELS[i]
                    e = (ex0, ex1)[i % 2][:].rearrange("p (n w) -> p n w", w=2 * h)
                    o = qk[:].rearrange("p (n w) -> p n w", w=2 * h)
                    kv = words(kT, 1024).rearrange("p (n w) -> p n w", w=2 * h)
                    qv = words(qT, 1024).rearrange("p (n w) -> p n w", w=2 * h)
                    dv.wait_ge(ev("level_exp"), l * 8 + (i + 1))
                    if i:
                        filled(dv, l, f"level{i - 1}")
                    V.tensor_tensor(o[:, :, 0:h], kv[:, :, 0:h], e[:, :, 0:h], ALU.mult)
                    V.tensor_tensor(o[:, :, h:2 * h], qv[:, :, h:2 * h], e[:, :, h:2 * h], ALU.mult).then_inc(ev("level_scaled"), 1)

                def keep_level(i):
                    p, n = unit(f"level{i}")
                    dv.wait_ge(ev(f"psum_full{p}"), l * PER_PAIR[p] + (n + 1))
                    take_wait()
                    V.copy_predicated(intra[:], levelmask[:, i:i + 1, :].broadcast_to([P, 8, P]),
                                      bank(f"level{i}")[:].rearrange("p (j t) -> p j t", j=8)).then_inc(taken_of(f"level{i}"), 1)
                diff(0)
                diff(1)
                taken(dv, l, "in0")
                for i in range(6):
                    scaled(i)
                    if i < 4:
                        dv.wait_ge(ev("level_scaled"), l * 6 + (i + 1))
                        diff(i + 2)
                    if i:
                        if i > 1:
                            taken(dv, l, f"level{i - 2}")
                        keep_level(i - 1)
                taken(dv, l, "level4")
                keep_level(5)
                taken(dv, l, "level5")
                keep_level(6)
                dv.wait_ge(ev("level_scaled"), l * 6 + 6)
                b16 = words(bT, 1024).rearrange("p (n w) -> p n w", w=CHUNK)
                V.tensor_tensor(ex1[:].rearrange("p (n w) -> p n w", w=CHUNK), b16, b16[:, :, CHUNK - 1:CHUNK].broadcast_to([P, 16, CHUNK]),
                                ALU.subtract).then_inc(ev("level_diff"), 1)
                dv.wait_ge(ev("level_exp"), l * 8 + 7)
                V.tensor_tensor(words(qT, 1024), words(qT, 1024), ex0[:], ALU.mult).then_inc(ev("qe_ready"), 1)
                dv.wait_ge(ev("level_exp"), l * 8 + 8)
                V.tensor_tensor(qk[:], words(kT, 1024), ex1[:], ALU.mult).then_inc(ev("kd_ready"), 1)
                taken(dv, l, "in3")
                dv.wait_ge(ev("hgain_loaded"), l * 16 + 16)
                link(V.tensor_tensor(sgtok[:], sgtok[:], hgain.unsqueeze(1).broadcast_to([P, TT, AW]), ALU.mult), l)
                dv.wait_ge(ev("decay"), l + 1)
                filled(dv, l, "U0")
                V.tensor_copy(state[:, 0].rearrange("p h d -> p (h d)"), bank("U0")[:, 0:AW]).then_inc(taken_of("U0"), 1)
                for c in (1, 2):
                    filled(dv, l, f"U{c}")
                    taken(dv, l, f"U{c - 1}")
                    for h in range(AH):
                        ins = V.scalar_tensor_tensor(out=state[:, c, h, :], in0=state[:, c - 1, h, :], scalar=dec[:, 4 * h + c:4 * h + c + 1],
                                                     in1=bank(f"U{c}")[:, h * P:(h + 1) * P], op0=ALU.mult, op1=ALU.add)
                    ins.then_inc(taken_of(f"U{c}"), 1)

                taken(dv, l, "in4"); taken(dv, l, "in5"); taken(dv, l, "in6"); taken(dv, l, "in7")
                x1, x2 = heads[:, :, :, 0:32], heads[:, :, :, 32:64]
                cb = cosT[:].unsqueeze(2).broadcast_to([P, TT, NHEADS, 32])
                sb_ = sinT[:].unsqueeze(2).broadcast_to([P, TT, NHEADS, 32])
                V.tensor_tensor(sin_x1, x1, sb_, ALU.mult)
                V.tensor_tensor(sin_x2, x2, sb_, ALU.mult)
                V.tensor_tensor(x1, x1, cb, ALU.mult)
                link(V.tensor_tensor(x2, x2, cb, ALU.mult), l)
                V.tensor_tensor(x1, x1, sin_x2, ALU.subtract)
                V.tensor_tensor(x2, x2, sin_x1, ALU.add).then_inc(ev("roped"), 1)

                dv.wait_ge(ev("o_squared"), l + 1)
                link(V.tensor_reduce(small[:, 0, :], ex0[:].rearrange("p (n w) -> p n w", w=P), AX_X, ALU.add), l)
                V.tensor_scalar(small[:, 0, :], small[:, 0, :], 1.0 / P, EPS, ALU.mult, ALU.add).then_inc(ev("o_var"), 1)
                dv.wait_ge(ev("o_root"), l + 1)
                link(V.reciprocal(small[:, 0, :], small[:, 1, :]), l)
                V.tensor_tensor(qk[:].rearrange("p (n w) -> p n w", w=P), bank("O")[:].rearrange("p (n w) -> p n w", w=P),
                                small[:, 0, :].unsqueeze(2).broadcast_to([P, 8, P]), ALU.mult).then_inc(taken_of("O"), 1)
                taken(dv, l, "O")
                V.tensor_tensor(qk[:], qk[:], words(sgtok, 1024), ALU.mult).then_inc(ev("ya_ready"), 1)

                for t, sc in ((0, score0), (1, score1)):
                    w = P * (t + 1)
                    taken(dv, l, f"index{t}")
                    link(V.tensor_scalar(sc[:], ex0[:, 0:w], iw[:, t, 0:1], None, ALU.mult), l)
                    for h in range(1, IH):
                        ins = V.scalar_tensor_tensor(out=sc[:], in0=ex0[:, PLACE[h] * w:(PLACE[h] + 1) * w], scalar=iw[:, t, h:h + 1], in1=sc[:], op0=ALU.mult, op1=ALU.add)
                        if h < IH - 1:
                            link(ins, l)
                    ins.then_inc(ev("score_summed"), 1)
                    dv.wait_ge(ev("score_summed"), l * 2 + (t + 1))
                    link(V.memset(sc[0:CHUNK, w - CHUNK:w], INADMISSIBLE), l, alone=True)
                for r in range(TOPK // 8):
                    for t, sc in ((0, score0), (1, score1)):
                        link(V.max(top8[:] if t else small[:, 7, :], sc[:]), l, alone=True)
                        link(V.match_replace(sc[:], top8[:] if t else small[:, 7, :], sc[:], CHOSEN), l, alone=True)
                for sc in (score0, score1):
                    link(V.tensor_scalar(sc[:], sc[:], -3.3e38, MASKED, ALU.is_gt, ALU.mult), l)

                def merge(x):
                    for i in range(2):
                        filled(dv, l, f"br{x}{i}")
                        taken(dv, l, f"g{x}{i}")
                        g_ = gate[:, 4 * i:4 * i + 4, :].rearrange("p k t -> p (k t)")
                        m_ = merged[:, 4 * i:4 * i + 4, :].rearrange("p k t -> p (k t)")
                        if x == "A":
                            V.tensor_tensor(m_, bank(f"br{x}{i}")[:], g_, ALU.mult).then_inc(taken_of(f"br{x}{i}"), 1)
                        else:
                            V.tensor_tensor(g_, bank(f"br{x}{i}")[:], g_, ALU.mult).then_inc(taken_of(f"br{x}{i}"), 1)
                            taken(dv, l, f"br{x}{i}")
                            ins = V.tensor_tensor(m_, m_, g_, ALU.add)
                            if x == "B":
                                ins.then_inc(ev("merged_B"), 1)
                            elif i == 1:
                                ins.then_inc(ev("merged"), 1)
                merge("A")

                def attention(x, bias):
                    def maxes(i):
                        hg_, t = GROUPS4[i]
                        w = P * (t + 1)
                        v = att[i % 2][:, 0:4 * w].rearrange("p (h s) -> p h s", h=4)
                        filled(dv, l, f"{x}S{i}")
                        for r in range(2):
                            ins = V.scalar_tensor_tensor(out=v[:, 2 * r:2 * r + 2, :], in0=bank(f"{x}S{i}")[:, 512 * r:512 * r + 2 * w].rearrange("p (m s) -> p m s", m=2),
                                                         scalar=HD ** -0.5, in1=bias[t].unsqueeze(1).broadcast_to([P, 2, w]), op0=ALU.mult, op1=ALU.add)
                        ins.then_inc(taken_of(f"{x}S{i}"), 1)
                        taken(dv, l, f"{x}S{i}")
                        mx = small[:, 2 + i % 2, 0:4]
                        link(V.tensor_reduce(mx, v, AX_X, ALU.max), l)
                        if x == "B":
                            sk = sinkc[:, 4 * hg_:4 * hg_ + 4].rearrange("p (m r) -> p r m", r=2)
                            by_head = lambda v: v.rearrange("p (r m) -> p r m", r=2)
                            link(V.tensor_tensor(by_head(mx), by_head(mx), sk, ALU.max), l)
                            link(V.tensor_tensor(by_head(small[:, 6 + i % 2, 0:4]), sk, by_head(mx), ALU.subtract), l)
                        V.tensor_scalar(mx, mx, -1.0, None, ALU.mult).then_inc(ev(f"max_{x}"), 1)

                    def normal(i):
                        hg_, t = GROUPS4[i]
                        w = P * (t + 1)
                        v = att[i % 2][:, 0:4 * w].rearrange("p (h s) -> p h s", h=4)
                        dv.wait_ge(ev(f"exp_{x}"), l * 4 + (i + 1))
                        sm = small[:, 4 + i % 2, 0:4]
                        if x == "B":
                            link(V.tensor_tensor(sm, sm, small[:, 6 + i % 2, 4:8], ALU.add), l)
                        link(V.reciprocal(sm, sm), l)
                        V.tensor_tensor(v, v, sm.unsqueeze(2).broadcast_to([P, 4, w]), ALU.mult).then_inc(ev(f"probs_{x}"), 1)
                    maxes(0); maxes(1); normal(0)
                    filled(dv, l, f"{x}T0"); maxes(2); normal(1)
                    filled(dv, l, f"{x}T1"); maxes(3); normal(2); normal(3)

                attention("B", (consts[:, C_B0:C_B0 + P], consts[:, C_B1:C_B1 + S]))
                merge("B")
                attention("C", (score0[:], score1[:]))
                merge("C")

                for i in range(2):
                    filled(dv, l, f"out{i}")
                    for j in range(4):
                        k = 4 * i + j
                        ins = V.scalar_tensor_tensor(out=xT[:, k, :], in0=bank(f"out{i}")[:, j * S:(j + 1) * S], scalar=mod[:, 16 + k:17 + k],
                                                     in1=xT[:, k, :], op0=ALU.mult, op1=ALU.add)
                    ins.then_inc(taken_of(f"out{i}"), 1)
                taken(dv, l, "out1")
                norm_unit(2, "norm2", gain2, 24)

                taken(dv, l, "router")
                g8 = lambda i: rg[:, i, :].rearrange("p (t g) -> p t g", t=TT)
                e32 = lambda i: rt[:, i, :].rearrange("p (n e) -> p n e", e=EG)
                one = lambda i: rg[:, i, :]
                lc = consts[:, C_LC:C_LC + NE].rearrange("p (g e) -> p g e", e=EG)
                lc = consts[:, C_LC:C_LC + NE].unsqueeze(1).broadcast_to([P, TT, NE])
                full_ = lambda i: rt[:, i, :].rearrange("p (t n) -> p t n", t=TT)
                bc4 = lambda i: one(i).unsqueeze(2).broadcast_to([P, TT * NG, EG])
                link(V.tensor_tensor(full_(0), aff[:], rb[:].unsqueeze(1).broadcast_to([P, TT, NE]), ALU.add), l)
                link(V.tensor_reduce(one(0), e32(0), AX_X, ALU.max), l)
                link(V.tensor_tensor(e32(1), e32(0), bc4(0), ALU.is_equal), l)
                link(V.tensor_tensor(full_(1), full_(1), lc, ALU.mult), l)
                link(V.tensor_reduce(one(1), e32(1), AX_X, ALU.max), l)
                link(V.tensor_tensor(e32(2), e32(1), bc4(1), ALU.is_equal), l)
                link(V.scalar_tensor_tensor(out=rt[:, 3, :], in0=rt[:, 2, :], scalar=MASKED, in1=rt[:, 0, :], op0=ALU.mult, op1=ALU.add), l)
                link(V.tensor_reduce(one(2), e32(3), AX_X, ALU.max), l)
                link(V.tensor_tensor(e32(4), e32(3), bc4(2), ALU.is_equal), l)
                link(V.tensor_tensor(full_(4), full_(4), lc, ALU.mult), l)
                link(V.tensor_reduce(one(3), e32(4), AX_X, ALU.max), l)
                link(V.tensor_tensor(e32(5), e32(4), bc4(3), ALU.is_equal), l)
                link(V.tensor_tensor(rt[:, 2, :], rt[:, 2, :], rt[:, 5, :], ALU.add), l)
                link(V.tensor_tensor(one(4), one(0), one(2), ALU.add), l)
                link(V.tensor_reduce(passes[:, 0:2], g8(4), AX_X, ALU.max), l)
                link(V.tensor_tensor(g8(5), g8(4), passes[:, 0:2].unsqueeze(2).broadcast_to([P, TT, NG]), ALU.is_equal), l)
                link(V.tensor_tensor(g8(5), g8(5), consts[:, C_GC:C_GC + NG].unsqueeze(1).broadcast_to([P, TT, NG]), ALU.mult), l)
                link(V.tensor_reduce(passes[:, 2:4], g8(5), AX_X, ALU.max), l)
                V.tensor_tensor(gsel[:], g8(5), passes[:, 2:4].unsqueeze(2).broadcast_to([P, TT, NG]), ALU.is_equal).then_inc(ev("group_chosen"), 1)
                dv.wait_ge(ev("group_chosen"), l + 1)
                link(V.tensor_tensor(e32(2), e32(2), gsel[:].rearrange("p t g -> p (t g)").unsqueeze(2).broadcast_to([P, TT * NG, EG]), ALU.mult), l)
                link(V.tensor_tensor(rt[:, 6, :], rt[:, 2, :], words(aff, TT * NE), ALU.mult), l)
                link(V.tensor_reduce(passes[:, 4:6], full_(6), AX_X, ALU.add), l)
                link(V.reciprocal(passes[:, 4:6], passes[:, 4:6]), l)
                link(V.tensor_tensor(comb[:], full_(6), passes[:, 4:6].unsqueeze(2).broadcast_to([P, TT, NE]), ALU.mult), l)
                filled(dv, l, "places")
                link(V.tensor_tensor(g8(6), bank("places")[:, 0:TT * NG].rearrange("p (t g) -> p t g", t=TT), gsel[:], ALU.mult), l)
                link(V.tensor_reduce(place[:], g8(6), AX_X, ALU.add), l)
                V.tensor_reduce(passes[:, 6:7], bank("places")[:, 2 * NG:3 * NG], AX_X, ALU.max).then_inc(taken_of("places"), 1)
                taken(dv, l, "places")
                link(V.tensor_scalar(passf[0:1, 3:4], passes[0:1, 6:7], float(CAP), 1.0, ALU.is_gt, ALU.add), l)
                for n in (2, 3):
                    link(V.scalar_tensor_tensor(out=passf[0:1, 3:4], in0=passes[0:1, 6:7], scalar=float(CAP * n), in1=passf[0:1, 3:4], op0=ALU.is_gt, op1=ALU.add), l)
                link(V.tensor_tensor(passf[0:1, bass.ds(l + 1, 1)], passf[0:1, bass.ds(l, 1)], passf[0:1, 3:4], ALU.add), l)
                V.tensor_copy(passi[0:1, bass.ds(l + 1, 1)], passf[0:1, bass.ds(l + 1, 1)]).then_inc(ev("pass_count"), 1)

                dv.wait_ge(ev("pass_count"), l + 2)
                done = dv.value_load(passi[0:1, bass.ds(l, 1)], min_val=0, max_val=8)
                end = dv.value_load(passi[0:1, bass.ds(l + 1, 1)], min_val=0, max_val=8)
                with dv.Fori(done, end) as t_:
                    for t in range(TT):
                        ins = V.tensor_scalar(one_hot[:, t, :], iota, place[:, t:t + 1], None, ALU.is_equal)
                    ins.then_inc(ev("one_hot"), 1)
                    dv.wait_ge(ev("one_hot"), t_ * 2 + 1)
                    V.tensor_scalar(place[:], place[:], -float(CAP), None, ALU.add).then_inc(ev("one_hot"), 1)
                    for t in range(TT):
                        ins = V.tensor_tensor(slots1[:, t], one_hot[:, t:t + 1, :].broadcast_to([P, NG, P]),
                                              gsel[:, t, :].unsqueeze(2).broadcast_to([P, NG, P]), ALU.mult)
                    ins.then_inc(ev("slots_ready"), 1)
                    dv.wait_ge(ev("one_hot"), t_ * 2 + 2)
                    dv.wait_ge(ev("slot_weights"), t_ + 1)
                    for j in range(2):
                        r = CAP * j
                        V.tensor_copy(wsel[r:r + CAP, :, :], psum[2][r:r + CAP, 0:NE].rearrange("p (g e r) -> p g e r", e=2, r=2)[:, :, :, j]).then_inc(ev("wsel_ready"), 1)
                    with dv.Fori(0, NG) as g:
                        dv.wait_ge(ev("wsel_ready"), t_ * 2 + 2)
                        dv.wait_ge(ev("gathered"), t_ * NG + g + 1)
                        V.tensor_copy(hg.rearrange("p k s -> p (k s)"), psum[0][:, 0:KD * CAP]).then_inc(ev("hg_ready"), 1)
                        for r in range(2):
                            dv.wait_ge(ev("silu_ready"), t_ * (2 * NG) + g * 2 + (r + 1))
                            V.scalar_tensor_tensor(out=he[:, r, :], in0=psum[1][:, 512 * r + FF:512 * r + 2 * FF], scalar=wsel[:, bass.ds(g, 1), r:r + 1].rearrange("p o r -> p (o r)"),
                                                   in1=silu_g[:, r, :], op0=ALU.mult, op1=ALU.mult).then_inc(ev("he_ready"), 1)
                        for i in range(2):
                            dv.wait_ge(ev("scattered"), t_ * (2 * NG) + g * 2 + (i + 1))
                            for j in range(4):
                                k = 4 * i + j
                                ins = V.scalar_tensor_tensor(out=xT[:, k, :], in0=psum[3][:, j * S:(j + 1) * S], scalar=mod[:, 40 + k:41 + k],
                                                             in1=xT[:, k, :], op0=ALU.mult, op1=ALU.add)
                            ins.then_inc(ev("scatter_added"), 1)
                        dv.wait_ge(ev("scatter_added"), t_ * (2 * NG) + g * 2 + 3)
                assert chain[0] == first + K_DVE, chain[0] - first

            dv.wait_ge(ev("final_sum"), 1)
            V.tensor_scalar(var[:], psum[0][:, 0:S], 1.0 / D, EPS, ALU.mult, ALU.add).then_inc(ev("var3"), 1)
            dv.wait_ge(ev("root3"), 1)
            V.reciprocal(var[:], rstd[:]).then_inc(ev("final_rstd"), 1)
            dv.wait_ge(ev("final_rstd"), 1)
            V.tensor_tensor(hT[:], xT[:], var[:].unsqueeze(1).broadcast_to([P, KD, S]), ALU.mult).then_inc(ev("final_rstd"), 1)
            dv.wait_ge(ev("final_rstd"), 2)
            for k in range(KD):
                ins = V.tensor_scalar(hT[:, k, :], hT[:, k, :], pcol[:, 40 + k:41 + k], None, ALU.mult)
            ins.then_inc(ev("final_ready"), 1)


NSMALL = 12


_INS = ["x", "c", "positions", "norm_attn_g", "norm_ffn_g", "w_ada", "b_ada", "w_in", "hgrn_lb_logits", "hgrn_norm_g",
        "attn_sinks", "w_branch_a", "w_branch_b", "w_branch_c", "w_out", "router_w", "router_b", "w_gate", "w_up",
        "w_down", "final_norm_g"]


def kernel(**inputs):
    import concourse.bacc as bacc
    from concourse.bass_utils import run_bass_kernel_spmd

    nc = bacc.Bacc("TRN2", target_bir_lowering=False, num_devices=1)
    arrays, aps = {}, {}
    given = {name: np.ascontiguousarray(inputs[name]) for name in _INS}
    given["constants"], given["level_masks"] = constants()
    for name, x in given.items():
        arrays[f"in_{name}"] = x
        aps[name] = nc.dram_tensor(f"in_{name}", x.shape, mybir.dt.from_np(x.dtype), kind="ExternalInput").ap()
    out = nc.dram_tensor("out_0", (1, S, D), F32, kind="ExternalOutput").ap()
    trunk(nc, aps, out)
    r = run_bass_kernel_spmd(nc, [arrays], core_ids=[0])
    return r.results[0]["out_0"]
```

```python
from contextlib import ExitStack

import numpy as np
import concourse.bass as bass
from concourse import mybir

F32 = mybir.dt.float32
I32 = mybir.dt.int32
U8 = mybir.dt.uint8
ACT = mybir.ActivationFunctionType
ALU = mybir.AluOpType
AX_X = mybir.AxisListType.X

P = 128
D = 1024
KD = D // P
S = 256
TT = S // P
DEPTH = 2
CHUNK = 64
AH = 4
AW = AH * P
NH = 8
HD = 64
IH = 4
TOPK = 64
NE = 32
NG = 8
EG = NE // NG
FF = 256
FB = FF // P
CAP = 64
LAYER_VISITS = NG + (S - NG) // CAP
MAX_VISITS = DEPTH * LAYER_VISITS
W_GATES = 3780
EPS = 1e-6
INADMISSIBLE = -3.0e38
CHOSEN = -3.4e38
MASKED = -1.0e30

HB_Q, HB_K, HC_Q, HC_K, HI_Q, HI_K, NHEADS = 0, 8, 12, 20, 22, 26, 28
NPAIR = NHEADS // 2
PB_Q, PB_K, PC_Q, PC_K, PI_Q, PI_K = (h // 2 for h in (HB_Q, HB_K, HC_Q, HC_K, HI_Q, HI_K))
LEVELS = [32, 16, 8, 4, 2, 1]

C_ID, C_ONE, C_UP, C_IOTA, C_B0, C_B1, C_KEEP, C_FREQ, C_GC, C_LC, C_PICK, C_EPS, NCONST = (
    0, 128, 256, 384, 512, 640, 896, 1152, 1184, 1192, 1224, 1225, 1226)

RING = 6
SLOT = 4096
ADA_FIRST = 4
GRANULES = ([f"ada{n}" for n in range(ADA_FIRST)] + [f"in{n}" for n in range(8)] + ["gA0", "gA1"]
            + [f"ada{n}" for n in range(ADA_FIRST, 12)] + ["wA", "gB0", "gB1", "wB", "gC0", "gC1", "wC", "out0", "out1"])
HOLES = (23, 26, 29, 31, 33)
PRE = 36
POS = [q for q in range(PRE) if q not in HOLES]
assert len(POS) == len(GRANULES) and PRE % RING == 0
NPRE = len(GRANULES)
PRE_FILLS = [sum(q % RING == s for q in POS) for s in range(RING)]


def granule(name):
    n = GRANULES.index(name)
    q = POS[n]
    before = [GRANULES[m] for m in range(n) if POS[m] % RING == q % RING]
    return q % RING, len(before) + 1, before[-1] if before else None


def last_granule(slot):
    return [GRANULES[m] for m in range(NPRE) if POS[m] % RING == slot][-1]


GROUPS4 = [(hg, t) for t in range(TT) for hg in range(2)]


def attention_units(x):
    return ([x + "S0", x + "S1", f"g{x}0"] + [x + u for u in ("T0", "S2", "V0", "T1", "S3", "V1")]
            + [f"g{x}1"] + [x + u for u in ("T2", "T3", "V2", "V3")])


UNITS = (["norm1"] + [f"ada{n}" for n in range(ADA_FIRST)] + [f"in{n}" for n in range(8)]
         + ["gA0", "gA1", "level0", "ada4", "level1", "ada5", "level2", "ada6", "level3", "ada7", "level4", "ada8",
            "level5", "level6", "ada9", "kdT", "ada10", "U0", "U1", "U2", "ada11", "O"]
         + [f"feat{i}" for i in range(4)] + ["yaT", "index0", "index1"]
         + ["brA0", "brA1"] + attention_units("B") + ["brB0", "brB1"]
         + attention_units("C") + ["brC0", "brC1", "out0", "out1", "norm2", "router", "h2tok0",
                                   "h2tok1", "places"])
PER_PAIR = [len(UNITS[p::4]) for p in range(4)]

TWO_PI_1 = 6.28125
TWO_PI_2 = float(np.float32(np.round((2 * np.pi - TWO_PI_1) * 2 ** 20) / 2 ** 20))
TWO_PI_3 = float(np.float32(2 * np.pi - TWO_PI_1 - TWO_PI_2))
ROUND = 12582912.0
PI_SAFE = 3.1415925

K_DVE = 136


def constants():
    c = np.zeros((P, NCONST), np.float32)
    r = np.arange(P)
    c[:, C_ID:C_ID + P] = np.eye(P)
    c[:, C_ONE:C_ONE + P] = 1.0
    c[:, C_UP:C_UP + P] = r[:, None] < r[None, :]
    c[:, C_IOTA:C_IOTA + P] = r[None, :] % CAP
    for t, at in ((0, C_B0), (1, C_B1)):
        keys = np.arange(P * (t + 1))[None, :] // CHUNK
        query = (P * t + r[:, None]) // CHUNK
        c[:, at:at + P * (t + 1)] = np.where((keys == query) | (keys == query - 1), 0.0, MASKED)
    c[:, C_KEEP:C_KEEP + S] = (np.arange(S) % CHUNK != 0)[None, :]
    c[:, C_FREQ:C_FREQ + 32] = np.float32(10000.0) ** (-np.arange(32, dtype=np.float32) * np.float32(2.0) / np.float32(HD))
    c[:, C_GC:C_GC + NG] = NG - np.arange(NG)
    c[:, C_LC:C_LC + NE] = EG - np.arange(NE) % EG
    c[::32, C_PICK] = 1.0
    c[:, C_EPS] = EPS
    m = np.zeros((P, 7, P), np.float32)
    s, t = r[:, None], r[None, :]
    for i, h in enumerate(LEVELS):
        m[:, i] = (s // (2 * h) == t // (2 * h)) & (s // h % 2 == 0) & (t // h % 2 == 1)
    m[:, 6] = s == t
    return c, m.reshape(P, 7 * P)


def trunk(nc, a, out):
    with ExitStack() as ctx:
        def sb(name, shape, dt=F32):
            return ctx.enter_context(nc.sbuf_tensor(name, shape, dt))

        events = {}

        def ev(name):
            if name not in events:
                events[name] = ctx.enter_context(nc.semaphore(name))
            return events[name]

        ring = sb("ring", [P, RING, SLOT])
        xT = sb("xT", [P, KD, S])
        hT = sb("hT", [P, KD, S])
        heads = sb("heads", [P, TT, NHEADS, HD])
        feat = sb("feat", [P, NPAIR, S])
        gate = sb("gate", [P, KD, S])
        qT = sb("qT", [P, AH, S])
        kT = sb("kT", [P, AH, S])
        bT = sb("bT", [P, AH, S])
        ex0 = sb("ex0", [P, 1024])
        ex1 = sb("ex1", [P, 1024])
        qk = sb("qk", [P, 1024])
        intra = sb("intra", [P, 8, P])
        vtok = sb("vtok", [P, TT, AW])
        sgtok = sb("sgtok", [P, TT, AW])
        state = sb("state", [P, 3, AH, P])
        consts = sb("consts", [P, NCONST])
        levelmask = sb("levelmask", [P, 7, P], U8)
        bv = sb("bv", [P, TT, 2, HD])
        cv = sb("cv", [P, TT, HD])
        iw = sb("iw", [P, TT, IH])
        cosT = sb("cosT", [P, TT, 32])
        sinT = sb("sinT", [P, TT, 32])
        posi = sb("posi", [P, TT], I32)
        posf = sb("posf", [P, TT])
        score0 = sb("score0", [P, P])
        score1 = sb("score1", [P, S])
        top8 = sb("top8", [P, 8])
        late_row = sb("late_row", [P, 512])
        spare = sb("spare", [P, 1])
        pcol = sb("pcol", [P, 160])
        lb = sb("lb", [P, 2, 2, AH])
        lbtmp = sb("lbtmp", [P, 6, AH])
        cond32 = sb("cond32", [P, KD, 32])
        cond = sb("cond", [P, KD])
        mod = sb("mod", [P, 48])
        cur = sb("cur", [P, 16 + 48 + 2 * AH])
        gain1 = sb("gain1", [P, KD])
        gain2 = sb("gain2", [P, KD])
        dec = sb("dec", [P, 16])
        small = sb("small", [P, 8, 8])
        sinks = sb("sinks", [P, DEPTH * NH])
        sinkc = sb("sinkc", [P, NH])
        rw = sb("rw", [P, KD, NE])
        rb = sb("rb", [P, NE])
        aff = sb("aff", [P, TT, NE])
        rg = sb("rg", [P, 8, TT * NG])
        gsel = sb("gsel", [P, TT, NG])
        comb = sb("comb", [P, TT, NE])
        place = sb("place", [P, TT])
        eight = sb("eight", [P, 8])
        visits = sb("visits", [1, DEPTH * NG + 1], I32)
        visitsf = sb("visitsf", [P, DEPTH * NG + 1])
        grouped = sb("grouped", [P, 2, NG])
        vmask = sb("vmask", [P, TT, MAX_VISITS + 1])
        vid = sb("vid", [P, TT])
        wsel = sb("wsel", [P, 2])
        comb4 = sb("comb4", [P, TT, EG])

        ident = consts[:, C_ID:C_ID + P]
        ones = consts[:, C_ONE:C_ONE + P]
        upper = consts[:, C_UP:C_UP + P]
        iota = consts[:, C_IOTA:C_IOTA + P]

        def words(ap, n, at=0):
            nd = len(ap.shape)
            if nd == 3:
                flat = ap[:].rearrange("p a b -> p (a b)")
            elif nd == 4:
                flat = ap[:].rearrange("p a b c -> p (a b c)")
            else:
                flat = ap[:]
            return flat[:, at:at + n]

        squares = words(heads, KD * S).rearrange("p (k t) -> p k t", k=KD)
        squares2 = words(feat, KD * S).rearrange("p (k t) -> p k t", k=KD)
        merged = words(heads, KD * S).rearrange("p (k t) -> p k t", k=KD)
        xtok = words(feat, TT * D).rearrange("p (t d) -> p t d", t=TT)
        h2tok = xtok
        sin_x1 = words(feat, TT * NHEADS * 32).rearrange("p (t h d) -> p t h d", t=TT, h=NHEADS)
        sin_x2 = words(feat, TT * NHEADS * 32, TT * NHEADS * 32).rearrange("p (t h d) -> p t h d", t=TT, h=NHEADS)
        yaT, ybT, ycT = bT, qT, kT
        adarow = [words(ex0, 512, 512 * (n % 2)) if n < ADA_FIRST else late_row[:] for n in range(12)]
        rt = words(ex0, 8 * TT * NE).rearrange("p (i n) -> p i n", i=8)
        one_hot = words(ex0, TT * P, 512).rearrange("p (t n) -> p t n", t=TT)
        var, rstd = words(ex1, S), words(ex1, S, S)
        ropetmp = words(ex1, 3 * TT * 32, 2 * S).rearrange("p (i t n) -> p i t n", i=3, t=TT)
        prow = words(ex1, 2 * P, 768).rearrange("p (i n) -> p i n", i=2)
        hgain = state[:, 2].rearrange("p h d -> p (h d)")
        att = [ex0[:], qk[:]]
        probT = [ex1[:], words(vtok, 1024)]
        slots1 = words(gate, TT * P).rearrange("p (t s) -> p t s", t=TT)
        slotsT = words(heads, S)
        hg = words(qT, KD * CAP).rearrange("p (k s) -> p k s", k=KD)
        silu_g = words(qT, 2 * FF, 512).rearrange("p (r f) -> p r f", r=2)
        he = words(kT, 2 * FF).rearrange("p (r f) -> p r f", r=2)
        heT = words(kT, 2 * FF, 512).rearrange("p (r f) -> p r f", r=2)
        yslot = words(bT, D)

        psum = [ctx.enter_context(nc.psum_tensor(f"pair{i}", [P, 1024], F32)) for i in range(4)]

        def unit(name):
            i = UNITS.index(name)
            return i % 4, i // 4

        def bank(name):
            return psum[unit(name)[0]]

        def filled(eng, l, name):
            p, n = unit(name)
            eng.wait_ge(ev(f"psum_full{p}"), l * PER_PAIR[p] + (n + 1))

        def taken(eng, l, name):
            p, n = unit(name)
            eng.wait_ge(ev(f"psum_taken{p}"), l * PER_PAIR[p] + (n + 2))

        def full_of(name):
            return ev(f"psum_full{unit(name)[0]}")

        def taken_of(name):
            return ev(f"psum_taken{unit(name)[0]}")

        PLACE = (0, 2, 1, 3)

        def score_halves(name, w):
            return bank(name)[:].rearrange("p (r n) -> p r n", r=2)[:, :, 0:2 * w]

        def slot3(name, k):
            return ring[:, granule(name)[0], :].rearrange("p (k n) -> p k n", k=k)

        def take_wait():
            nc.vector.memset(spare[:], 0.0)

        block = ctx.enter_context(nc.Block())

        @block.sync
        def _(sp):
            sp.sem_inc(ev("hidden_full"), 2)
            sp.sem_inc(ev("down_done"), 2)
            for p in range(4):
                sp.sem_inc(ev(f"psum_taken{p}"), 1)
            sp.sem_inc(ev("scatter_added"), 1)

            def fetch(slot, parts):
                for dst, src in parts:
                    sp.dma_start(dst, src).then_inc(ev(f"landed{slot}"), 16)

            def cols(w, l, lo, n, slot):
                src = w[bass.ds(l, 1), :, lo:lo + n].rearrange("o (k p) n -> p (o k) n", p=P)
                dst = ring[:, slot, 0:KD * n].rearrange("p (k n) -> p k n", k=KD)
                return [(dst[:, 4 * i:4 * i + 4, :], src[:, 4 * i:4 * i + 4, :]) for i in range(2)]

            def rows(w, l, slot):
                src = w[bass.ds(l, 1)].rearrange("o (k p) n -> p (o k) n", p=P)
                dst = ring[:, slot, :].rearrange("p (k n) -> p k n", k=4)
                return [(dst[:, 2 * i:2 * i + 2, :], src[:, 2 * i:2 * i + 2, :]) for i in range(2)]

            def expert_parts(l, g):
                for e in range(EG):
                    dst = ring[:, e, :].rearrange("p (k n) -> p k n", k=KD)
                    yield e, [(dst[:, :, u * FF:(u + 1) * FF],
                               a[w][bass.ds(l, 1), bass.ds(g * EG + e, 1)].rearrange("a b (k p) n -> p (a b k) n", p=P))
                              for u, w in enumerate(("w_gate", "w_up"))]
                for r in range(2):
                    dst = ring[:, EG + r, :].rearrange("p (e k n) -> p e k n", e=2, k=FB)
                    yield EG + r, [(dst[:, e], a["w_down"][bass.ds(l, 1), bass.ds(g * EG + 2 * r + e, 1)]
                                    .rearrange("a b (k p) n -> p (a b k) n", p=P)) for e in range(2)]

            def wait_expert_slot(slot, pair_count):
                name = "hidden_full" if slot < EG else "down_done"
                sp.wait_ge(ev(name), pair_count + (slot // 2 if slot < EG else slot - EG) + 1)

            def wait_reader(l, name):
                if name.startswith("ada"):
                    sp.wait_ge(ev("ada_rows"), l * 12 + (int(name[3:]) + 1))
                else:
                    filled(sp, l, f"br{name[1]}1" if name[0] == "w" else name)

            first_loads = ((consts[:], a["constants"]), (prow[0:8, 0, :], a["c"].rearrange("o (k p) -> (o k) p", p=P)),
                           (prow[8:24, 0, :], a["norm_attn_g"].rearrange("o (k p) -> (o k) p", p=P)),
                           (prow[24:40, 0, :], a["norm_ffn_g"].rearrange("o (k p) -> (o k) p", p=P)),
                           (prow[40:48, 0, :], a["final_norm_g"].rearrange("(k p) -> k p", p=P)),
                           (prow[48:56, 0, :], a["hgrn_lb_logits"].rearrange("o (k p) -> (o k) p", p=P)),
                           (prow[0:96, 1, :], a["b_ada"].rearrange("o (k p) -> (o k) p", p=P)))
            assert len(first_loads) == NFIRST
            for dst, src in first_loads:
                sp.dma_start(dst, src).then_inc(ev("params_loaded"), 16)

            with sp.Fori(0, DEPTH) as l:
                sp.wait_ge(ev("visits_counted"), l + 1)
                done = sp.value_load(visits[0:1, bass.ds(l * NG, 1)], min_val=0, max_val=MAX_VISITS)
                for name in GRANULES:
                    slot, _, before = granule(name)
                    if before is None:
                        wait_expert_slot(slot, done * 2)
                    else:
                        wait_reader(l, before)
                    if name.startswith("ada"):
                        fetch(slot, cols(a["w_ada"], l, 512 * int(name[3:]), 512, slot))
                    elif name.startswith("in"):
                        i = int(name[2:])
                        fetch(slot, cols(a["w_in"], l, 512 * i, min(512, W_GATES - 512 * i), slot))
                    elif name[0] == "g":
                        fetch(slot, cols(a["w_in"], l, W_GATES + D * "ABC".index(name[1]) + 512 * int(name[2]), 512, slot))
                    elif name[0] == "w":
                        fetch(slot, rows(a["w_branch_" + name[1].lower()], l, slot))
                    else:
                        fetch(slot, cols(a["w_out"], l, 512 * int(name[3:]), 512, slot))
                for slot, parts in expert_parts(l, 0):
                    wait_reader(l, last_granule(slot))
                    fetch(slot, parts)
                with sp.Fori(1, NG) as g:
                    sp.wait_ge(ev("visits_counted"), l + 2)
                    ahead = sp.value_load(visits[0:1, bass.ds(l * NG + g, 1)], min_val=0, max_val=MAX_VISITS)
                    for slot, parts in expert_parts(l, g):
                        wait_expert_slot(slot, ahead * 2)
                        fetch(slot, parts)
            sp.wait_ge(ev("out_stored"), 32)

        @block.gpsimd
        def _(gp):
            n = [0]

            def load(dst, src, **how):
                gp.dma_start(dst, src, **how).then_inc(ev("small_loaded"), 16)
                n[0] += 1
            for t in range(TT):
                gp.dma_start(xtok[:, t, :], a["x"][0, P * t:P * t + P, :]).then_inc(ev("x_loaded"), 16)
            load(qk[:, 0:7 * P], a["level_masks"])
            load(posi[:], a["positions"].rearrange("o (t p) -> p (o t)", p=P), allow_slow_non_contiguous=True)
            load(sinks[:], a["attn_sinks"].rearrange("l h -> (l h)").partition_broadcast(P))
            load(rb[:], a["router_b"].partition_broadcast(P))
            load(rw[:], a["router_w"].rearrange("(k p) n -> p k n", p=P))
            assert n[0] == NSMALL
            gp.memset(words(intra, 1024), 0.0).then_inc(ev("intra_zeroed"), 1)
            with gp.Fori(0, DEPTH) as l:
                gp.wait_ge(ev("visits_counted"), l + 1)
                gp.dma_start(hgain, a["hgrn_norm_g"][bass.ds(l, 1), :].rearrange("o n -> (o n)").partition_broadcast(P)).then_inc(ev("hgain_loaded"), 16)

        @block.tensor
        def _(pe):
            mm = nc.tensor.matmul
            tr = nc.tensor.transpose
            order = [0]

            def claim(l, name):
                assert UNITS[order[0] % len(UNITS)] == name, (UNITS[order[0]], name)
                order[0] += 1
                p, n = unit(name)
                pe.wait_ge(ev(f"psum_taken{p}"), l * PER_PAIR[p] + (n + 1))
                return psum[p]

            def landed(l, name):
                slot, fills, _ = granule(name)
                pe.wait_ge(ev(f"landed{slot}"), l * (32 * (PRE_FILLS[slot] + NG)) + 32 * fills)

            pe.wait_ge(ev("params_loaded"), 16 * NFIRST)
            tr(psum[2][:, 0:56], prow[0:56, 0, :], ident[0:56, 0:56])
            tr(psum[2][:, 64:160], prow[0:96, 1, :], ident[0:96, 0:96]).then_inc(ev("params_turned"), 1)
            pe.wait_ge(ev("x_loaded"), 16 * TT)
            for i in range(2):
                for k in range(4):
                    for t in range(TT):
                        m = tr(psum[i][:, k * S + t * P:k * S + t * P + P], xtok[:, t, (4 * i + k) * P:(4 * i + k + 1) * P], ident)
                m.then_inc(ev("x_turned"), 1)
            pe.wait_ge(ev("x_ready"), 2)
            pe.wait_ge(ev("params_ready"), 1)
            pe.wait_ge(ev("cond_ready"), 1)

            def norm_sum(dst, done_sem, sq_sem, base, squares=squares):
                for k in range(KD):
                    if k % 4 == 0:
                        pe.wait_ge(ev(sq_sem), base + (k // 4 + 1))
                    m = mm(dst[:, 0:S], ones, squares[:, k, :], start=k == 0, stop=k == KD - 1)
                m.then_inc(done_sem, 1)

            def cols_unit(l, name, rhs, kn):
                w = slot3(name, KD)
                dst = claim(l, name)
                for j in range(4):
                    for k in range(kn):
                        m = mm(dst[:, j * S:(j + 1) * S], w[:, k, j * P:(j + 1) * P], rhs[:, k, :], start=k == 0, stop=k == kn - 1)
                return m

            with pe.Fori(0, DEPTH) as l:
                pe.wait_ge(ev("visits_counted"), l + 1)
                done = pe.value_load(visits[0:1, bass.ds(l * NG, 1)], min_val=0, max_val=MAX_VISITS)

                def ada_columns(n):
                    taken_row = ev("ada_row")
                    pe.wait_ge(taken_row, l * 12 + (n + 1))
                    dst = bank(f"ada{n}")
                    for j in range(4):
                        m = mm(dst[:, 512 + j:513 + j], adarow[n][:, j * P:(j + 1) * P], consts[:, C_PICK:C_PICK + 1], start=True, stop=True)
                    m.then_inc(full_of(f"ada{n}"), 1)

                def ada_rows(n):
                    landed(l, f"ada{n}")
                    w = slot3(f"ada{n}", KD)
                    dst = claim(l, f"ada{n}")
                    for k in range(2):
                        for j in range(4):
                            m = mm(dst[32 * j:32 * j + 32, 0:512], cond32[:, 2 * j + k, :], w[:, 2 * j + k, :], start=k == 0, stop=k == 1)
                    m.then_inc(ev("ada_rows"), 1)
                norm_sum(claim(l, "norm1"), full_of("norm1"), "squared1", l * 2)
                for n in range(ADA_FIRST):
                    ada_rows(n)
                    if n:
                        ada_columns(n - 1)
                ada_columns(ADA_FIRST - 1)

                pe.wait_ge(ev("h1_dve"), l + 1)
                pe.wait_ge(ev("h1_act"), l + 1)
                for i in range(8):
                    name = f"in{i}"
                    landed(l, name)
                    if i < 2:
                        m = cols_unit(l, name, hT, KD)
                    else:
                        n = min(512, W_GATES - 512 * i)
                        w = ring[:, granule(name)[0], 0:KD * n].rearrange("p (k n) -> p k n", k=KD)
                        dst = claim(l, name)
                        for t in range(TT):
                            for k in range(KD):
                                m = mm(dst[:, 512 * t:512 * t + n], hT[:, k, t * P:t * P + P], w[:, k, :], start=k == 0, stop=k == KD - 1)
                    m.then_inc(full_of(name), 1)

                def gates(x, i):
                    name = f"g{x}{i}"
                    landed(l, name)
                    cols_unit(l, name, hT, KD).then_inc(full_of(name), 1)
                gates("A", 0)
                gates("A", 1)

                for i in range(7):
                    dst = claim(l, f"level{i}")
                    if i < 6:
                        pe.wait_ge(ev("level_scaled"), l * 6 + (i + 1))
                    for j in range(8):
                        lhs = words(kT, P, j * P) if i == 6 else qk[:, j * P:(j + 1) * P]
                        rhs = words(qT, P, j * P) if i == 6 else qk[:, j * P:(j + 1) * P]
                        m = mm(dst[:, j * P:(j + 1) * P], lhs, rhs, start=True, stop=True)
                    m.then_inc(full_of(f"level{i}"), 1)
                    if i != 5:
                        n = ADA_FIRST + i if i < 5 else 9
                        ada_rows(n)
                        if n > ADA_FIRST:
                            ada_columns(n - 1)
                dst = claim(l, "kdT")
                pe.wait_ge(ev("kd_ready"), l + 1)
                for j in range(8):
                    m = tr(dst[:, j * P:(j + 1) * P], qk[:, j * P:(j + 1) * P], ident)
                m.then_inc(full_of("kdT"), 1)
                ada_rows(10)
                ada_columns(9)
                taken(pe, l, "kdT")
                taken(pe, l, "in2")
                for c in range(3):
                    dst = claim(l, f"U{c}")
                    r = CHUNK * (c % 2)
                    for h in range(AH):
                        at = (2 * h + c // 2) * P
                        m = mm(dst[:, h * P:(h + 1) * P], ex1[r:r + CHUNK, at:at + P], vtok[r:r + CHUNK, c // 2, h * P:(h + 1) * P], start=True, stop=True)
                    m.then_inc(full_of(f"U{c}"), 1)
                    if c == 1:
                        ada_columns(10)
                ada_rows(11)
                dst = claim(l, "O")
                taken(pe, l, "level6")
                pe.wait_ge(ev("qe_ready"), l + 1)
                taken(pe, l, "U2")
                for t in range(TT):
                    for h in range(AH):
                        o = 512 * t + h * P
                        m = mm(dst[:, o:o + P], intra[:, 2 * h + t, :], vtok[:, t, h * P:(h + 1) * P], start=True, stop=False, skip_group_check=True)
                        for c in ((1,) if t == 0 else (2, 3)):
                            r = CHUNK * (c % 2)
                            m = mm(dst[r:r + CHUNK, o:o + P], qT[:, h, c * CHUNK:(c + 1) * CHUNK], state[:, c - 1, h, :], start=False, stop=True, skip_group_check=True)
                m.then_inc(full_of("O"), 1)
                ada_columns(11)
                for i in range(4):
                    dst = claim(l, f"feat{i}")
                    if i == 0:
                        pe.wait_ge(ev("roped"), l + 1)
                    for p in range(4 * i, min(4 * i + 4, NPAIR)):
                        for t in range(TT):
                            src = heads[:, t, 2 * p:2 * p + 2, :].rearrange("p h d -> p (h d)")
                            m = tr(dst[:, (p % 4) * S + t * P:(p % 4) * S + t * P + P], src, ident)
                    m.then_inc(full_of(f"feat{i}"), 1)
                dst = claim(l, "yaT")
                pe.wait_ge(ev("ya_ready"), l + 1)
                for t in range(TT):
                    for h in range(AH):
                        m = tr(dst[:, h * S + t * P:h * S + t * P + P], qk[:, 512 * t + h * P:512 * t + h * P + P], ident)
                m.then_inc(full_of("yaT"), 1)

                for i in range(4):
                    taken(pe, l, f"feat{i}")
                for t in range(TT):
                    w = P * (t + 1)
                    dst = claim(l, f"index{t}")
                    for h in range(IH):
                        r = HD * (h % 2)
                        at = 512 * (h % 2) + (h // 2) * w
                        m = mm(dst[:, at:at + w], feat[r:r + HD, PI_Q + h // 2, t * P:t * P + P], feat[r:r + HD, PI_K, 0:w], start=True, stop=True)
                    m.then_inc(full_of(f"index{t}"), 1)

                def branch(x, y):
                    landed(l, f"w{x}")
                    w = slot3(f"w{x}", 4)
                    for i in range(2):
                        dst = claim(l, f"br{x}{i}")
                        for j in range(4):
                            for k in range(4):
                                m = mm(dst[:, j * S:(j + 1) * S], w[:, k, (4 * i + j) * P:(4 * i + j + 1) * P], y[:, k, :], start=k == 0, stop=k == 3)
                        m.then_inc(full_of(f"br{x}{i}"), 1)

                taken(pe, l, "yaT")
                branch("A", yaT)

                def attention(x, qp, kp, values):
                    def scores(i):
                        hg_, t = GROUPS4[i]
                        w = P * (t + 1)
                        dst = claim(l, f"{x}S{i}")
                        for j in range(4):
                            h = 4 * hg_ + j
                            r = HD * (h % 2)
                            at = 512 * (j % 2) + (j // 2) * w
                            m = mm(dst[:, at:at + w], feat[r:r + HD, qp + h // 2, t * P:t * P + P], feat[r:r + HD, kp(h), 0:w], start=True, stop=True)
                        m.then_inc(full_of(f"{x}S{i}"), 1)

                    def turn(i):
                        _, t = GROUPS4[i]
                        dst = claim(l, f"{x}T{i}")
                        pe.wait_ge(ev(f"probs_{x}"), l * 4 + (i + 1))
                        for j in range(4 * (t + 1)):
                            m = tr(dst[:, j * P:(j + 1) * P], att[i % 2][:, j * P:(j + 1) * P], ident)
                        m.then_inc(full_of(f"{x}T{i}"), 1)

                    def weigh(i):
                        _, t = GROUPS4[i]
                        dst = claim(l, f"{x}V{i}")
                        taken(pe, l, f"{x}T{i}")
                        for j in range(4):
                            r = HD * (j % 2)
                            for kt in range(t + 1):
                                m = mm(dst[r:r + HD, (j // 2) * P:(j // 2 + 1) * P], values(4 * GROUPS4[i][0] + j, kt),
                                       probT[i % 2][:, (PLACE[j] * (t + 1) + kt) * P:(PLACE[j] * (t + 1) + kt + 1) * P], start=kt == 0, stop=kt == t)
                        m.then_inc(full_of(f"{x}V{i}"), 1)
                    scores(0); scores(1); gates(x, 0)
                    turn(0); scores(2); weigh(0)
                    turn(1); scores(3); weigh(1); gates(x, 1)
                    turn(2); turn(3); weigh(2); weigh(3)
                    taken(pe, l, f"{x}V2")
                    taken(pe, l, f"{x}V3")

                attention("B", PB_Q, lambda h: PB_K + h // 4, lambda h, kt: bv[:, kt, h // 4, :])
                branch("B", ybT)
                attention("C", PC_Q, lambda h: PC_K, lambda h, kt: cv[:, kt, :])
                branch("C", ycT)

                pe.wait_ge(ev("merged"), l + 1)
                for i in range(2):
                    landed(l, f"out{i}")
                    cols_unit(l, f"out{i}", merged, KD).then_inc(full_of(f"out{i}"), 1)

                norm_sum(claim(l, "norm2"), full_of("norm2"), "squared2", l * 2, squares2)
                pe.wait_ge(ev("h2_dve"), l + 1)
                pe.wait_ge(ev("h2_act"), l + 1)
                dst = claim(l, "router")
                for t in range(TT):
                    for k in range(KD):
                        m = mm(dst[:, t * NE:(t + 1) * NE], hT[:, k, t * P:t * P + P], rw[:, k, :], start=k == 0, stop=k == KD - 1)
                m.then_inc(full_of("router"), 1)
                for t in range(TT):
                    dst = claim(l, f"h2tok{t}")
                    for k in range(KD):
                        m = tr(dst[:, k * P:(k + 1) * P], hT[:, k, t * P:t * P + P], ident)
                    m.then_inc(full_of(f"h2tok{t}"), 1)
                dst = claim(l, "places")
                pe.wait_ge(ev("group_chosen"), l + 1)
                mm(dst[:, 0:NG], upper, gsel[:, 0, :], start=True, stop=True)
                mm(dst[:, NG:2 * NG], ones, gsel[:, 0, :], start=True, stop=False)
                mm(dst[:, NG:2 * NG], upper, gsel[:, 1, :], start=False, stop=True)
                mm(dst[:, 2 * NG:3 * NG], ones, gsel[:, 0, :], start=True, stop=False)
                mm(dst[:, 2 * NG:3 * NG], ones, gsel[:, 1, :], start=False, stop=True).then_inc(full_of("places"), 1)

                for p in range(4):
                    pe.wait_ge(ev(f"psum_taken{p}"), l * PER_PAIR[p] + (PER_PAIR[p] + 1))
                pe.wait_ge(ev("visits_counted"), l + 2)
                last = pe.value_load(visits[0:1, bass.ds(l * NG + NG, 1)], min_val=0, max_val=MAX_VISITS)
                with pe.Fori(0, NG) as g:
                    start = pe.value_load(visits[0:1, bass.ds(l * NG + g, 1)], min_val=0, max_val=MAX_VISITS)
                    end = pe.value_load(visits[0:1, bass.ds(l * NG + g + 1, 1)], min_val=0, max_val=MAX_VISITS)
                    with pe.Fori(start, end) as v:
                        pe.wait_ge(ev("slots_ready"), v + l + 1)
                        for k in range(KD):
                            for t in range(TT):
                                m = mm(psum[0][:, k * CAP:(k + 1) * CAP], h2tok[:, t, k * P:(k + 1) * P], slots1[:, t, 0:CAP], start=t == 0, stop=t == TT - 1)
                        m.then_inc(ev("gathered"), 1)
                        for t in range(TT):
                            m = tr(psum[0][:, 768 + t * P:768 + (t + 1) * P], slots1[:, t, :], ident)
                        for t in range(TT):
                            m = mm(psum[2][:, 0:EG], slots1[:, t, :], comb4[:, t, :], start=t == 0, stop=t == TT - 1)
                        m.then_inc(ev("slots_used"), 1)
                        pe.wait_ge(ev("hg_ready"), v + 1)

                        def arrived(slot):
                            pe.wait_ge(ev(f"landed{slot}"), l * (32 * (PRE_FILLS[slot] + NG)) + g * 32 + (32 * PRE_FILLS[slot] + 32))

                        pe.wait_ge(ev("scatter_added"), v * 2 + 1)
                        for r in range(2):
                            arrived(2 * r)
                            arrived(2 * r + 1)
                            for k in range(KD):
                                for j in range(2):
                                    w = ring[:, 2 * r + j, :].rearrange("p (k n) -> p k n", k=KD)
                                    m = mm(psum[1][CAP * j:CAP * j + CAP, 512 * r:512 * r + 512], hg[:, k, :], w[:, k, :], start=k == 0, stop=k == KD - 1)
                            m.then_inc(ev("hidden_full"), 1)
                        for r in range(2):
                            pe.wait_ge(ev("he_ready"), v * 2 + (r + 1))
                            for f in range(FB):
                                m = tr(psum[0][:, 512 + f * P:512 + (f + 1) * P], he[:, r, f * P:(f + 1) * P], ident)
                            m.then_inc(ev("he_turned"), 1)
                            pe.wait_ge(ev("heT_ready"), v * 2 + (r + 1))
                            arrived(EG + r)
                            w = ring[:, EG + r, :].rearrange("p (e k n) -> p e k n", e=2, k=FB)
                            for f in range(FB):
                                for half in range(2):
                                    for j in range(2):
                                        m = mm(psum[2][CAP * j:CAP * j + CAP, 512 * half:512 * half + 512], heT[:, r, f * P + CAP * j:f * P + CAP * j + CAP],
                                               w[:, j, f, 512 * half:512 * half + 512], start=(r == 0 and f == 0), stop=(r == 1 and f == FB - 1))
                            m.then_inc(ev("down_done"), 1)
                        pe.wait_ge(ev("yslot_ready"), v * 2 + 2)
                        pe.wait_ge(ev("slotsT_ready"), v + 1)
                        for i in range(2):
                            if i == 0:
                                pe.wait_ge(ev("scatter_added"), v * 2 + 1)
                            for j in range(4):
                                m = mm(psum[3 - 2 * i][:, j * S:(j + 1) * S], yslot[:, (4 * i + j) * P:(4 * i + j + 1) * P],
                                       slotsT, start=True, stop=True)
                            m.then_inc(ev("scattered"), 1)
                pe.wait_ge(ev("scatter_added"), last * 2 + 1)

            norm_sum(psum[0], ev("final_sum"), "squared3", 0)
            pe.wait_ge(ev("final_ready"), 1)
            for t in range(TT):
                for k in range(KD):
                    m = tr(psum[1 + t][:, k * P:(k + 1) * P], hT[:, k, t * P:t * P + P], ident)
                m.then_inc(ev("final_turned"), 1)

        @block.scalar
        def _(ac):
            act = nc.scalar.activation
            ac.wait_ge(ev("params_ready"), 1)
            act(cond[:], pcol[:, 0:KD], ACT.Silu).then_inc(ev("cond_silu"), 1)
            ac.wait_ge(ev("lb_shifted"), 1)
            act(lbtmp[:, 3:5, :], lbtmp[:, 1:3, :], ACT.Exp).then_inc(ev("lb_exp"), 1)
            ac.wait_ge(ev("x_ready"), 2)

            def squares_of_x(name, squares=squares, wait_half=None):
                for i in range(2):
                    if wait_half:
                        wait_half(i)
                    act(squares[:, 4 * i:4 * i + 4, :], xT[:, 4 * i:4 * i + 4, :], ACT.Square).then_inc(ev(name), 1)

            with ac.Fori(0, DEPTH) as l:
                ac.wait_ge(ev("visits_counted"), l + 1)
                done = ac.value_load(visits[0:1, bass.ds(l * NG, 1)], min_val=0, max_val=MAX_VISITS)
                ac.wait_ge(ev("scatter_added"), done * 2 + 1)
                squares_of_x("squared1")

                def ada_row(n):
                    p, _ = unit(f"ada{n}")
                    ac.wait_ge(ev("ada_rows"), l * 12 + (n + 1))
                    before = n - 2 if n < ADA_FIRST else n - 1
                    if before >= (0 if n < ADA_FIRST else ADA_FIRST):
                        filled(ac, l, f"ada{before}")
                    act(adarow[n], psum[p][:, 0:512], ACT.Copy).then_inc(ev("ada_row"), 1)
                def root(src, dst, ready, name, l1):
                    ac.wait_ge(ev(ready), l1)
                    act(dst, src, ACT.Sqrt).then_inc(ev(name), 1)

                def modulate(which, l1, shift, gain):
                    ac.wait_ge(ev(f"h{which}_scaled"), l1)
                    if which == 1:
                        ac.wait_ge(ev("gain1_ready"), l1)
                    for k in range(4, KD):
                        ins = act(hT[:, k, :], hT[:, k, :], ACT.Identity, bias=mod[:, shift + k:shift + k + 1], scale=gain[:, k:k + 1])
                    ins.then_inc(ev(f"h{which}_act"), 1)
                root(var[:], rstd[:], "var1", "root1", l + 1)
                for n in range(ADA_FIRST):
                    ada_row(n)
                modulate(1, l + 1, 0, gain1)

                filled(ac, l, "in0")
                act(words(qT, 1024), bank("in0")[:], ACT.Silu).then_inc(taken_of("in0"), 1)
                filled(ac, l, "in1")
                act(ex0[:], bank("in1")[:], ACT.Sigmoid).then_inc(taken_of("in1"), 1)
                ac.wait_ge(ev("angles"), l * 2 + 1)
                act(sinT[:], ropetmp[:, 1], ACT.Sin).then_inc(ev("rope_table"), 1)
                ac.wait_ge(ev("angles"), l * 2 + 2)
                act(cosT[:], ropetmp[:, 2], ACT.Sin).then_inc(ev("rope_table"), 1)
                filled(ac, l, "in2")
                act(words(vtok, 1024), bank("in2")[:], ACT.Copy).then_inc(taken_of("in2"), 1)
                filled(ac, l, "in3")
                act(words(sgtok, 1024), bank("in3")[:], ACT.Silu).then_inc(taken_of("in3"), 1)
                ac.wait_ge(ev("f_ready"), l + 1)
                act(qk[:], ex0[:], ACT.Ln).then_inc(ev("logf"), 1)

                def by_token(name, lo, n):
                    return bank(name)[:].rearrange("p (t n) -> p t n", t=TT)[:, :, lo:lo + n]

                def to_heads(name, lo, h, n, step=1):
                    src = by_token(name, lo, n * HD).rearrange("p t (h d) -> p t h d", h=n)
                    return act(heads[:, :, h:h + (n - 1) * step + 1:step, :], src, ACT.Copy)
                filled(ac, l, "in4")
                to_heads("in4", 0, HB_Q, 8).then_inc(taken_of("in4"), 1)
                filled(ac, l, "in5")
                to_heads("in5", 0, HB_K, 2, 2)
                to_heads("in5", 0, HB_K + 1, 2, 2)
                act(bv[:].rearrange("p t h d -> p t (h d)"), by_token("in5", 128, 128), ACT.Copy)
                to_heads("in5", 256, HC_Q, 4).then_inc(taken_of("in5"), 1)
                filled(ac, l, "in6")
                to_heads("in6", 0, HC_Q + 4, 4)
                to_heads("in6", 256, HC_K, 1)
                to_heads("in6", 256, HC_K + 1, 1)
                act(cv[:], by_token("in6", 320, HD), ACT.Copy)
                to_heads("in6", 384, HI_Q, 2).then_inc(taken_of("in6"), 1)
                filled(ac, l, "in7")
                to_heads("in7", 0, HI_Q + 2, 2)
                to_heads("in7", 128, HI_K, 1)
                to_heads("in7", 128, HI_K + 1, 1)
                act(iw[:], by_token("in7", 192, IH), ACT.Copy).then_inc(taken_of("in7"), 1)


                def gates(x, i):
                    filled(ac, l, f"g{x}{i}")
                    if x == "B":
                        taken(ac, l, f"brA{i}")
                    if x == "C":
                        ac.wait_ge(ev("merged_B"), l * 2 + (i + 1))
                    act(gate[:, 4 * i:4 * i + 4, :].rearrange("p k t -> p (k t)"), bank(f"g{x}{i}")[:], ACT.Sigmoid).then_inc(taken_of(f"g{x}{i}"), 1)
                for i, h in enumerate(LEVELS):
                    ex = (ex0, ex1)[i % 2]
                    ac.wait_ge(ev("level_diff"), l * 7 + (i + 1))
                    v = ex[:].rearrange("p (n w) -> p n w", w=2 * h)
                    act(v[:, :, 0:h], v[:, :, 0:h], ACT.Exp, scale=-1.0)
                    act(v[:, :, h:2 * h], v[:, :, h:2 * h], ACT.Exp).then_inc(ev("level_exp"), 1)
                    if i == 1:
                        gates("A", 0)
                        gates("A", 1)
                    if i:
                        ada_row(ADA_FIRST + i - 1)
                ac.wait_ge(ev("level_scaled"), l * 6 + 5)
                act(ex0[:], words(bT, 1024), ACT.Exp).then_inc(ev("level_exp"), 1)
                act(dec[:], words(bT, 1024).rearrange("p (n w) -> p n w", w=CHUNK)[:, :, CHUNK - 1], ACT.Exp).then_inc(ev("decay"), 1)
                ac.wait_ge(ev("level_diff"), l * 7 + 7)
                act(ex1[:], ex1[:], ACT.Exp, scale=-1.0).then_inc(ev("level_exp"), 1)
                ada_row(9)
                filled(ac, l, "kdT")
                act(ex1[:], bank("kdT")[:], ACT.Copy).then_inc(taken_of("kdT"), 1)
                ada_row(10)
                ada_row(11)
                filled(ac, l, "O")
                ac.wait_ge(ev("qe_ready"), l + 1)
                act(ex0[:], bank("O")[:], ACT.Square).then_inc(ev("o_squared"), 1)
                ac.wait_ge(ev("o_var"), l + 1)
                act(small[:, 1, :], small[:, 0, :], ACT.Sqrt).then_inc(ev("o_root"), 1)

                for i in range(4):
                    n = min(4, NPAIR - 4 * i) * S
                    filled(ac, l, f"feat{i}")
                    act(words(feat, n, 1024 * i), bank(f"feat{i}")[:, 0:n], ACT.Copy).then_inc(taken_of(f"feat{i}"), 1)
                filled(ac, l, "yaT")
                act(words(yaT, 1024), bank("yaT")[:], ACT.Copy).then_inc(taken_of("yaT"), 1)
                for t in range(TT):
                    filled(ac, l, f"index{t}")
                    if t:
                        ac.wait_ge(ev("score_summed"), l * 2 + 1)
                    w = P * (t + 1)
                    act(ex0[:, 0:4 * w].rearrange("p (r n) -> p r n", r=2), score_halves(f"index{t}", w), ACT.Relu).then_inc(taken_of(f"index{t}"), 1)

                def attention(x, yT):
                    def exps(i):
                        hg_, t = GROUPS4[i]
                        w = P * (t + 1)
                        ac.wait_ge(ev(f"max_{x}"), l * 4 + (i + 1))
                        for j in range(4):
                            ins = act(att[i % 2][:, j * w:(j + 1) * w], att[i % 2][:, j * w:(j + 1) * w], ACT.Exp,
                                      bias=small[:, 2 + i % 2, j:j + 1], accum_out=small[:, 4 + i % 2, j:j + 1])
                        if x == "B":
                            ins = act(small[:, 6 + i % 2, 4:8], small[:, 6 + i % 2, 0:4], ACT.Exp)
                        ins.then_inc(ev(f"exp_{x}"), 1)

                    def out_of(kind, i):
                        hg_, t = GROUPS4[i]
                        name = f"{x}{kind}{i}"
                        filled(ac, l, name)
                        if kind == "T":
                            n = 512 * (t + 1)
                            act(probT[i % 2][:, 0:n], bank(name)[:, 0:n], ACT.Copy).then_inc(taken_of(name), 1)
                        else:
                            act(yT[:, 2 * hg_:2 * hg_ + 2, t * P:t * P + P], bank(name)[:, 0:2 * P].rearrange("p (k t) -> p k t", k=2),
                                ACT.Copy).then_inc(taken_of(name), 1)
                    exps(0); exps(1)
                    out_of("T", 0); gates(x, 0); out_of("V", 0); out_of("T", 1)
                    exps(2); exps(3); out_of("V", 1)
                    gates(x, 1); out_of("T", 2); out_of("T", 3); out_of("V", 2); out_of("V", 3)

                attention("B", ybT)
                attention("C", ycT)

                squares_of_x("squared2", squares2, lambda i: taken(ac, l, f"out{i}"))
                root(var[:], rstd[:], "var2", "root2", l + 1)
                modulate(2, l + 1, 24, gain2)
                filled(ac, l, "router")
                act(words(aff, TT * NE), bank("router")[:, 0:TT * NE], ACT.Sigmoid).then_inc(taken_of("router"), 1)
                for t in range(TT):
                    filled(ac, l, f"h2tok{t}")
                    act(h2tok[:, t, :], bank(f"h2tok{t}")[:], ACT.Copy).then_inc(taken_of(f"h2tok{t}"), 1)

                ac.wait_ge(ev("visits_counted"), l + 2)
                end = ac.value_load(visits[0:1, bass.ds(l * NG + NG, 1)], min_val=0, max_val=MAX_VISITS)
                with ac.Fori(done, end) as v:
                    ac.wait_ge(ev("slots_used"), v + 1)
                    act(slotsT, psum[0][:, 768:1024], ACT.Copy).then_inc(ev("slotsT_ready"), 1)
                    for r in range(2):
                        ac.wait_ge(ev("hidden_full"), v * 2 + (r + 3))
                        act(silu_g[:, r, :], psum[1][:, 512 * r:512 * r + FF], ACT.Silu).then_inc(ev("silu_ready"), 1)
                    for r in range(2):
                        ac.wait_ge(ev("he_turned"), v * 2 + (r + 1))
                        act(heT[:, r, :], psum[0][:, 512:512 + FF], ACT.Copy).then_inc(ev("heT_ready"), 1)
                    ac.wait_ge(ev("down_done"), v * 2 + 4)
                    act(yslot[:, 0:512], psum[2][:, 0:512], ACT.Copy).then_inc(ev("yslot_ready"), 1)

            done = ac.value_load(visits[0:1, DEPTH * NG:DEPTH * NG + 1], min_val=0, max_val=MAX_VISITS)
            ac.wait_ge(ev("scatter_added"), done * 2 + 1)
            squares_of_x("squared3")
            root(var[:], rstd[:], "var3", "root3", 1)
            for t in range(TT):
                ac.wait_ge(ev("final_turned"), t + 1)
                act(h2tok[:, t, :], psum[1 + t][:], ACT.Copy).then_inc(ev("final_copied"), 1)
                ac.wait_ge(ev("final_copied"), t + 1)
                ac.dma_start(out[0, P * t:P * t + P, :], h2tok[:, t, :]).then_inc(ev("out_stored"), 16)

        @block.vector
        def _(dv):
            V = nc.vector
            chain = [0]

            def link(ins, l=0, alone=False):
                chain[0] += 1
                ins.then_inc(ev("dve_chain"), 1)
                dv.wait_ge(ev("dve_chain"), l * K_DVE + chain[0])
                if alone:
                    take_wait()

            link(V.memset(visits[:], 0))
            V.memset(visitsf[:], 0.0).then_inc(ev("visits_counted"), 1)
            dv.wait_ge(ev("params_turned"), 1)
            link(V.tensor_copy(pcol[:, 0:56], psum[2][:, 0:56]))
            V.tensor_copy(pcol[:, 64:160], psum[2][:, 64:160]).then_inc(ev("params_ready"), 1)
            for i in range(2):
                dv.wait_ge(ev("x_turned"), i + 1)
                V.tensor_copy(xT[:, 4 * i:4 * i + 4, :].rearrange("p k t -> p (k t)"), psum[i][:]).then_inc(ev("x_ready"), 1)
            dv.wait_ge(ev("params_ready"), 1)
            dv.wait_ge(ev("cond_silu"), 1)
            V.tensor_copy(cond32[:], cond[:].unsqueeze(2).broadcast_to([P, KD, 32])).then_inc(ev("cond_ready"), 1)
            z0, z1 = pcol[:, 48:52], pcol[:, 52:56]
            link(V.tensor_tensor(lbtmp[:, 0, :], z0, z1, ALU.max))
            link(V.tensor_tensor(lbtmp[:, 1, :], z0, lbtmp[:, 0, :], ALU.subtract))
            V.tensor_tensor(lbtmp[:, 2, :], z1, lbtmp[:, 0, :], ALU.subtract).then_inc(ev("lb_shifted"), 1)
            dv.wait_ge(ev("small_loaded"), 16 * NSMALL)
            V.tensor_copy(words(levelmask, 7 * P), qk[:, 0:7 * P])
            dv.wait_ge(ev("lb_exp"), 1)
            link(V.tensor_tensor(lbtmp[:, 0, :], lbtmp[:, 3, :], lbtmp[:, 4, :], ALU.add))
            link(V.reciprocal(lbtmp[:, 5, :], lbtmp[:, 0, :]))
            link(V.tensor_tensor(lbtmp[:, 3, :], lbtmp[:, 3, :], lbtmp[:, 5, :], ALU.mult))
            link(V.tensor_tensor(lbtmp[:, 4, :], lbtmp[:, 4, :], lbtmp[:, 5, :], ALU.mult))
            link(V.tensor_tensor(lbtmp[:, 4, :], lbtmp[:, 3, :], lbtmp[:, 4, :], ALU.add))
            link(V.tensor_tensor(lb[:, 0, 0, :], lbtmp[:, 3, :], lbtmp[:, 3, :], ALU.subtract))
            link(V.tensor_tensor(lb[:, 1, 0, :], lbtmp[:, 4, :], lbtmp[:, 3, :], ALU.subtract))
            for i in range(2):
                link(V.tensor_scalar(lb[:, i, 1, :], lb[:, i, 0, :], -1.0, 1.0, ALU.mult, ALU.add))
            link(V.memset(small[:], 0.0))
            first = chain[0]
            dv.wait_ge(ev("intra_zeroed"), 1)

            with dv.Fori(0, DEPTH) as l:
                dv.wait_ge(ev("visits_counted"), l + 1)
                done = dv.value_load(visits[0:1, bass.ds(l * NG, 1)], min_val=0, max_val=MAX_VISITS)
                V.tensor_copy(cur[:, 0:8], pcol[:, bass.ds(l * 8 + 8, 8)])
                V.tensor_copy(cur[:, 8:16], pcol[:, bass.ds(l * 8 + 24, 8)])
                V.tensor_copy(cur[:, 16:64], pcol[:, bass.ds(l * 48 + 64, 48)])
                V.tensor_copy(sinkc[:], sinks[:, bass.ds(l * NH, NH)])
                link(V.tensor_copy(cur[:, 64:72], lb[:, bass.ds(l, 1)].rearrange("p o a h -> p (o a h)")), l)
                lbc, omc = cur[:, 64:68], cur[:, 68:72]
                def ada_column(n):
                    p, _ = unit(f"ada{n}")
                    filled(dv, l, f"ada{n}")
                    V.tensor_tensor(mod[:, 4 * n:4 * n + 4], psum[p][:, 512:516], cur[:, 16 + 4 * n:20 + 4 * n], ALU.add).then_inc(ev(f"psum_taken{p}"), 1)

                def norm_unit(which, name, gain, shift, modulation=None):
                    filled(dv, l, name)
                    V.tensor_scalar(var[:], bank(name)[:, 0:S], 1.0 / D, EPS, ALU.mult, ALU.add).then_inc(ev(f"var{which}"), 1)
                    dv.wait_ge(ev(f"root{which}"), l + 1)
                    link(V.reciprocal(var[:], rstd[:]), l)
                    V.tensor_tensor(hT[:, 4:8, :], xT[:, 4:8, :], var[:].unsqueeze(1).broadcast_to([P, 4, S]), ALU.mult).then_inc(ev(f"h{which}_scaled"), 1)
                    V.tensor_tensor(hT[:, 0:4, :], xT[:, 0:4, :], var[:].unsqueeze(1).broadcast_to([P, 4, S]), ALU.mult).then_inc(taken_of(name), 1)
                    if modulation:
                        modulation()
                    taken(dv, l, name)
                    for k in range(4):
                        ins = V.tensor_scalar(hT[:, k, :], hT[:, k, :], gain[:, k:k + 1], mod[:, shift + k:shift + k + 1], ALU.mult, ALU.add)
                    ins.then_inc(ev(f"h{which}_dve"), 1)

                def first_modulation():
                    for n in range(ADA_FIRST):
                        ada_column(n)
                    taken(dv, l, "ada2")
                    taken(dv, l, "ada3")
                    V.scalar_tensor_tensor(out=gain1[:], in0=mod[:, 8:16], scalar=1.0, in1=cur[:, 0:8], op0=ALU.add, op1=ALU.mult).then_inc(ev("gain1_ready"), 1)
                    dv.wait_ge(ev("gain1_ready"), l + 1)
                norm_unit(1, "norm1", gain1, 0, first_modulation)

                link(V.tensor_copy(posf[:], posi[:]), l)
                for t in range(TT):
                    link(V.tensor_scalar(ropetmp[:, 0, t, :], consts[:, C_FREQ:C_FREQ + 32], posf[:, t:t + 1], None, ALU.mult), l)
                for i, (turn, back) in enumerate(((0.0, 0.0), (0.25, np.pi / 2))):
                    r, n = ropetmp[:, 1 + i], (sinT, cosT)[i]
                    link(V.tensor_scalar(n[:], ropetmp[:, 0], 1.0 / (2 * np.pi), turn, ALU.mult, ALU.add), l)
                    link(V.tensor_scalar(n[:], n[:], ROUND, None, ALU.add), l)
                    link(V.tensor_scalar(n[:], n[:], -ROUND, None, ALU.add), l)
                    link(V.scalar_tensor_tensor(out=r, in0=n[:], scalar=-TWO_PI_1, in1=ropetmp[:, 0], op0=ALU.mult, op1=ALU.add), l)
                    link(V.scalar_tensor_tensor(out=r, in0=n[:], scalar=-TWO_PI_2, in1=r, op0=ALU.mult, op1=ALU.add), l)
                    link(V.scalar_tensor_tensor(out=r, in0=n[:], scalar=-TWO_PI_3, in1=r, op0=ALU.mult, op1=ALU.add), l)
                    link(V.tensor_scalar(r, r, float(back), PI_SAFE, ALU.add, ALU.min), l)
                    V.tensor_scalar(r, r, -PI_SAFE, None, ALU.max).then_inc(ev("angles"), 1)

                taken(dv, l, "in1")
                f = ex0[:].rearrange("p (h t) -> p h t", h=AH)
                for h in range(AH):
                    ins = V.tensor_scalar(f[:, h, :], f[:, h, :], omc[:, h:h + 1], lbc[:, h:h + 1], ALU.mult, ALU.add)
                    if h == AH - 1:
                        link(ins, l)
                    else:
                        ins
                link(V.tensor_scalar(words(kT, 1024), ex0[:], -1.0, 1.0, ALU.mult, ALU.add), l)
                V.tensor_scalar(ex0[:], ex0[:], 2.0 ** -64, None, ALU.max).then_inc(ev("f_ready"), 1)
                dv.wait_ge(ev("logf"), l + 1)
                for h in range(AH):
                    ins = V.tensor_tensor_scan(bT[:, h, :], consts[:, C_KEEP:C_KEEP + S], qk[:, h * S:(h + 1) * S], 0.0, ALU.mult, ALU.add)
                link(ins, l)

                def diff(i):
                    h = LEVELS[i]
                    v = words(bT, 1024).rearrange("p (n w) -> p n w", w=2 * h)
                    ex = (ex0, ex1)[i % 2][:].rearrange("p (n w) -> p n w", w=2 * h)
                    V.tensor_tensor(ex, v, v[:, :, h - 1:h].broadcast_to([P, 512 // h, 2 * h]), ALU.subtract).then_inc(ev("level_diff"), 1)

                def scaled(i):
                    h = LEVELS[i]
                    e = (ex0, ex1)[i % 2][:].rearrange("p (n w) -> p n w", w=2 * h)
                    o = qk[:].rearrange("p (n w) -> p n w", w=2 * h)
                    kv = words(kT, 1024).rearrange("p (n w) -> p n w", w=2 * h)
                    qv = words(qT, 1024).rearrange("p (n w) -> p n w", w=2 * h)
                    dv.wait_ge(ev("level_exp"), l * 8 + (i + 1))
                    if i:
                        filled(dv, l, f"level{i - 1}")
                    V.tensor_tensor(o[:, :, 0:h], kv[:, :, 0:h], e[:, :, 0:h], ALU.mult)
                    V.tensor_tensor(o[:, :, h:2 * h], qv[:, :, h:2 * h], e[:, :, h:2 * h], ALU.mult).then_inc(ev("level_scaled"), 1)

                def keep_level(i):
                    p, n = unit(f"level{i}")
                    dv.wait_ge(ev(f"psum_full{p}"), l * PER_PAIR[p] + (n + 1))
                    take_wait()
                    V.copy_predicated(intra[:], levelmask[:, i:i + 1, :].broadcast_to([P, 8, P]),
                                      bank(f"level{i}")[:].rearrange("p (j t) -> p j t", j=8)).then_inc(taken_of(f"level{i}"), 1)
                diff(0)
                dv.wait_ge(ev("rope_table"), l * 2 + 2)
                diff(1)
                taken(dv, l, "in0")
                for i in range(6):
                    scaled(i)
                    if i < 4:
                        dv.wait_ge(ev("level_scaled"), l * 6 + (i + 1))
                        diff(i + 2)
                    if i:
                        if i > 1:
                            taken(dv, l, f"level{i - 2}")
                        keep_level(i - 1)
                    if i > 1:
                        ada_column(i + 2)
                dv.wait_ge(ev("level_scaled"), l * 6 + 6)
                b16 = words(bT, 1024).rearrange("p (n w) -> p n w", w=CHUNK)
                V.tensor_tensor(ex1[:].rearrange("p (n w) -> p n w", w=CHUNK), b16, b16[:, :, CHUNK - 1:CHUNK].broadcast_to([P, 16, CHUNK]),
                                ALU.subtract).then_inc(ev("level_diff"), 1)
                taken(dv, l, "level4")
                keep_level(5)
                taken(dv, l, "level5")
                keep_level(6)
                ada_column(8)
                dv.wait_ge(ev("level_exp"), l * 8 + 7)
                V.tensor_tensor(words(qT, 1024), words(qT, 1024), ex0[:], ALU.mult).then_inc(ev("qe_ready"), 1)
                dv.wait_ge(ev("level_exp"), l * 8 + 8)
                V.tensor_tensor(qk[:], words(kT, 1024), ex1[:], ALU.mult).then_inc(ev("kd_ready"), 1)
                taken(dv, l, "in3")
                dv.wait_ge(ev("hgain_loaded"), l * 16 + 16)
                link(V.tensor_tensor(sgtok[:], sgtok[:], hgain.unsqueeze(1).broadcast_to([P, TT, AW]), ALU.mult), l)
                dv.wait_ge(ev("decay"), l + 1)
                ada_column(9)
                filled(dv, l, "U0")
                V.tensor_copy(state[:, 0].rearrange("p h d -> p (h d)"), bank("U0")[:, 0:AW]).then_inc(taken_of("U0"), 1)
                for c in (1, 2):
                    filled(dv, l, f"U{c}")
                    taken(dv, l, f"U{c - 1}")
                    for h in range(AH):
                        ins = V.scalar_tensor_tensor(out=state[:, c, h, :], in0=state[:, c - 1, h, :], scalar=dec[:, 4 * h + c:4 * h + c + 1],
                                                     in1=bank(f"U{c}")[:, h * P:(h + 1) * P], op0=ALU.mult, op1=ALU.add)
                    ins.then_inc(taken_of(f"U{c}"), 1)
                ada_column(10)

                taken(dv, l, "in4"); taken(dv, l, "in5"); taken(dv, l, "in6"); taken(dv, l, "in7")
                x1, x2 = heads[:, :, :, 0:32], heads[:, :, :, 32:64]
                cb = cosT[:].unsqueeze(2).broadcast_to([P, TT, NHEADS, 32])
                sb_ = sinT[:].unsqueeze(2).broadcast_to([P, TT, NHEADS, 32])
                V.tensor_tensor(sin_x1, x1, sb_, ALU.mult)
                V.tensor_tensor(sin_x2, x2, sb_, ALU.mult)
                V.tensor_tensor(x1, x1, cb, ALU.mult)
                link(V.tensor_tensor(x2, x2, cb, ALU.mult), l)
                V.tensor_tensor(x1, x1, sin_x2, ALU.subtract)
                V.tensor_tensor(x2, x2, sin_x1, ALU.add).then_inc(ev("roped"), 1)

                ada_column(11)
                dv.wait_ge(ev("o_squared"), l + 1)
                link(V.tensor_reduce(small[:, 0, :], ex0[:].rearrange("p (n w) -> p n w", w=P), AX_X, ALU.add), l)
                V.tensor_scalar(small[:, 0, :], small[:, 0, :], 1.0 / P, EPS, ALU.mult, ALU.add).then_inc(ev("o_var"), 1)
                dv.wait_ge(ev("o_root"), l + 1)
                link(V.reciprocal(small[:, 0, :], small[:, 1, :]), l)
                V.tensor_tensor(qk[:].rearrange("p (n w) -> p n w", w=P), bank("O")[:].rearrange("p (n w) -> p n w", w=P),
                                small[:, 0, :].unsqueeze(2).broadcast_to([P, 8, P]), ALU.mult).then_inc(taken_of("O"), 1)
                taken(dv, l, "O")
                V.tensor_tensor(qk[:], qk[:], words(sgtok, 1024), ALU.mult).then_inc(ev("ya_ready"), 1)
                for n in (8, 9, 10, 11):
                    taken(dv, l, f"ada{n}")
                link(V.scalar_tensor_tensor(out=gain2[:], in0=mod[:, 32:40], scalar=1.0, in1=cur[:, 8:16], op0=ALU.add, op1=ALU.mult), l)

                for t, sc in ((0, score0), (1, score1)):
                    w = P * (t + 1)
                    taken(dv, l, f"index{t}")
                    link(V.tensor_scalar(sc[:], ex0[:, 0:w], iw[:, t, 0:1], None, ALU.mult), l)
                    for h in range(1, IH):
                        ins = V.scalar_tensor_tensor(out=sc[:], in0=ex0[:, PLACE[h] * w:(PLACE[h] + 1) * w], scalar=iw[:, t, h:h + 1], in1=sc[:], op0=ALU.mult, op1=ALU.add)
                        if h < IH - 1:
                            link(ins, l)
                    ins.then_inc(ev("score_summed"), 1)
                    dv.wait_ge(ev("score_summed"), l * 2 + (t + 1))
                    link(V.memset(sc[0:CHUNK, w - CHUNK:w], INADMISSIBLE), l, alone=True)

                def largest(rounds):
                    for r in rounds:
                        for t, sc in ((0, score0), (1, score1)):
                            link(V.max(top8[:] if t else eight[:], sc[:]), l, alone=True)
                            link(V.match_replace(sc[:], top8[:] if t else eight[:], sc[:], CHOSEN), l, alone=True)
                largest(range(0, TOPK // 16))

                def merge(x):
                    for i in range(2):
                        filled(dv, l, f"br{x}{i}")
                        taken(dv, l, f"g{x}{i}")
                        g_ = gate[:, 4 * i:4 * i + 4, :].rearrange("p k t -> p (k t)")
                        m_ = merged[:, 4 * i:4 * i + 4, :].rearrange("p k t -> p (k t)")
                        if x == "A":
                            V.tensor_tensor(m_, bank(f"br{x}{i}")[:], g_, ALU.mult).then_inc(taken_of(f"br{x}{i}"), 1)
                        else:
                            V.tensor_tensor(g_, bank(f"br{x}{i}")[:], g_, ALU.mult).then_inc(taken_of(f"br{x}{i}"), 1)
                            taken(dv, l, f"br{x}{i}")
                            ins = V.tensor_tensor(m_, m_, g_, ALU.add)
                            if x == "B":
                                ins.then_inc(ev("merged_B"), 1)
                            elif i == 1:
                                ins.then_inc(ev("merged"), 1)
                merge("A")

                def attention(x, bias, meanwhile=None):
                    def maxes(i):
                        hg_, t = GROUPS4[i]
                        w = P * (t + 1)
                        v = att[i % 2][:, 0:4 * w].rearrange("p (h s) -> p h s", h=4)
                        filled(dv, l, f"{x}S{i}")
                        for r in range(2):
                            ins = V.scalar_tensor_tensor(out=v[:, 2 * r:2 * r + 2, :], in0=bank(f"{x}S{i}")[:, 512 * r:512 * r + 2 * w].rearrange("p (m s) -> p m s", m=2),
                                                         scalar=HD ** -0.5, in1=bias[t].unsqueeze(1).broadcast_to([P, 2, w]), op0=ALU.mult, op1=ALU.add)
                        ins.then_inc(taken_of(f"{x}S{i}"), 1)
                        taken(dv, l, f"{x}S{i}")
                        mx = small[:, 2 + i % 2, 0:4]
                        link(V.tensor_reduce(mx, v, AX_X, ALU.max), l)
                        if x == "B":
                            sk = sinkc[:, 4 * hg_:4 * hg_ + 4].rearrange("p (m r) -> p r m", r=2)
                            by_head = lambda v: v.rearrange("p (r m) -> p r m", r=2)
                            link(V.tensor_tensor(by_head(mx), by_head(mx), sk, ALU.max), l)
                            link(V.tensor_tensor(by_head(small[:, 6 + i % 2, 0:4]), sk, by_head(mx), ALU.subtract), l)
                        V.tensor_scalar(mx, mx, -1.0, None, ALU.mult).then_inc(ev(f"max_{x}"), 1)

                    def normal(i):
                        hg_, t = GROUPS4[i]
                        w = P * (t + 1)
                        v = att[i % 2][:, 0:4 * w].rearrange("p (h s) -> p h s", h=4)
                        dv.wait_ge(ev(f"exp_{x}"), l * 4 + (i + 1))
                        sm = small[:, 4 + i % 2, 0:4]
                        if x == "B":
                            link(V.tensor_tensor(sm, sm, small[:, 6 + i % 2, 4:8], ALU.add), l)
                        link(V.reciprocal(sm, sm), l)
                        V.tensor_tensor(v, v, sm.unsqueeze(2).broadcast_to([P, 4, w]), ALU.mult).then_inc(ev(f"probs_{x}"), 1)
                    maxes(0); maxes(1); normal(0); normal(1)
                    if meanwhile:
                        meanwhile()
                    filled(dv, l, f"{x}T0"); maxes(2)
                    filled(dv, l, f"{x}T1"); maxes(3); normal(2); normal(3)

                def rest_of_largest():
                    largest(range(TOPK // 16, TOPK // 8))
                    for sc in (score0, score1):
                        link(V.tensor_scalar(sc[:], sc[:], -3.3e38, MASKED, ALU.is_gt, ALU.mult), l)
                attention("B", (consts[:, C_B0:C_B0 + P], consts[:, C_B1:C_B1 + S]), rest_of_largest)
                merge("B")
                attention("C", (score0[:], score1[:]))
                merge("C")

                for i in range(2):
                    filled(dv, l, f"out{i}")
                    for j in range(4):
                        k = 4 * i + j
                        ins = V.scalar_tensor_tensor(out=xT[:, k, :], in0=bank(f"out{i}")[:, j * S:(j + 1) * S], scalar=mod[:, 16 + k:17 + k],
                                                     in1=xT[:, k, :], op0=ALU.mult, op1=ALU.add)
                    ins.then_inc(taken_of(f"out{i}"), 1)
                taken(dv, l, "out1")
                norm_unit(2, "norm2", gain2, 24)

                taken(dv, l, "router")
                g8 = lambda i: rg[:, i, :].rearrange("p (t g) -> p t g", t=TT)
                e32 = lambda i: rt[:, i, :].rearrange("p (n e) -> p n e", e=EG)
                one = lambda i: rg[:, i, :]
                lc = consts[:, C_LC:C_LC + NE].rearrange("p (g e) -> p g e", e=EG)
                lc = consts[:, C_LC:C_LC + NE].unsqueeze(1).broadcast_to([P, TT, NE])
                full_ = lambda i: rt[:, i, :].rearrange("p (t n) -> p t n", t=TT)
                bc4 = lambda i: one(i).unsqueeze(2).broadcast_to([P, TT * NG, EG])
                link(V.tensor_tensor(full_(0), aff[:], rb[:].unsqueeze(1).broadcast_to([P, TT, NE]), ALU.add), l)
                link(V.tensor_reduce(one(0), e32(0), AX_X, ALU.max), l)
                link(V.tensor_tensor(e32(1), e32(0), bc4(0), ALU.is_equal), l)
                link(V.tensor_tensor(full_(1), full_(1), lc, ALU.mult), l)
                link(V.tensor_reduce(one(1), e32(1), AX_X, ALU.max), l)
                link(V.tensor_tensor(e32(2), e32(1), bc4(1), ALU.is_equal), l)
                link(V.scalar_tensor_tensor(out=rt[:, 3, :], in0=rt[:, 2, :], scalar=MASKED, in1=rt[:, 0, :], op0=ALU.mult, op1=ALU.add), l)
                link(V.tensor_reduce(one(2), e32(3), AX_X, ALU.max), l)
                link(V.tensor_tensor(e32(4), e32(3), bc4(2), ALU.is_equal), l)
                link(V.tensor_tensor(full_(4), full_(4), lc, ALU.mult), l)
                link(V.tensor_reduce(one(3), e32(4), AX_X, ALU.max), l)
                link(V.tensor_tensor(e32(5), e32(4), bc4(3), ALU.is_equal), l)
                link(V.tensor_tensor(rt[:, 2, :], rt[:, 2, :], rt[:, 5, :], ALU.add), l)
                link(V.tensor_tensor(one(4), one(0), one(2), ALU.add), l)
                link(V.tensor_reduce(eight[:, 0:2], g8(4), AX_X, ALU.max), l)
                link(V.tensor_tensor(g8(5), g8(4), eight[:, 0:2].unsqueeze(2).broadcast_to([P, TT, NG]), ALU.is_equal), l)
                link(V.tensor_tensor(g8(5), g8(5), consts[:, C_GC:C_GC + NG].unsqueeze(1).broadcast_to([P, TT, NG]), ALU.mult), l)
                link(V.tensor_reduce(eight[:, 2:4], g8(5), AX_X, ALU.max), l)
                V.tensor_tensor(gsel[:], g8(5), eight[:, 2:4].unsqueeze(2).broadcast_to([P, TT, NG]), ALU.is_equal).then_inc(ev("group_chosen"), 1)
                dv.wait_ge(ev("group_chosen"), l + 1)
                link(V.tensor_tensor(e32(2), e32(2), gsel[:].rearrange("p t g -> p (t g)").unsqueeze(2).broadcast_to([P, TT * NG, EG]), ALU.mult), l)
                link(V.tensor_tensor(rt[:, 6, :], rt[:, 2, :], words(aff, TT * NE), ALU.mult), l)
                link(V.tensor_reduce(eight[:, 4:6], full_(6), AX_X, ALU.add), l)
                link(V.reciprocal(eight[:, 4:6], eight[:, 4:6]), l)
                link(V.tensor_tensor(comb[:], full_(6), eight[:, 4:6].unsqueeze(2).broadcast_to([P, TT, NE]), ALU.mult), l)
                link(V.tensor_reduce(comb4[:], comb[:].rearrange("p t (g e) -> p t e g", e=EG), AX_X, ALU.add), l)
                filled(dv, l, "places")
                link(V.tensor_scalar(grouped[:, 0, :], bank("places")[:, 2 * NG:3 * NG], float(CAP), 1.0, ALU.is_gt, ALU.add), l)
                for n in (2, 3):
                    link(V.scalar_tensor_tensor(out=grouped[:, 0, :], in0=bank("places")[:, 2 * NG:3 * NG], scalar=float(CAP * n), in1=grouped[:, 0, :], op0=ALU.is_gt, op1=ALU.add), l)
                link(V.tensor_tensor_scan(grouped[:, 1, :], ones[:, 0:NG], grouped[:, 0, :], 0.0, ALU.mult, ALU.add), l)
                link(V.tensor_scalar(visitsf[:, bass.ds(l * NG + 1, NG)], grouped[:, 1, :], visitsf[:, bass.ds(l * NG, 1)], None, ALU.add), l)
                V.tensor_copy(visits[0:1, bass.ds(l * NG + 1, NG)], visitsf[0:1, bass.ds(l * NG + 1, NG)]).then_inc(ev("visits_counted"), 1)
                link(V.tensor_tensor(g8(6), bank("places")[:, 0:TT * NG].rearrange("p (t g) -> p t g", t=TT), gsel[:], ALU.mult), l)
                V.tensor_reduce(place[:], g8(6), AX_X, ALU.add).then_inc(taken_of("places"), 1)
                taken(dv, l, "places")
                link(V.tensor_tensor(g8(7), gsel[:], visitsf[:, bass.ds(l * NG, NG)].unsqueeze(1).broadcast_to([P, TT, NG]), ALU.mult), l)
                link(V.tensor_reduce(vid[:], g8(7), AX_X, ALU.add), l)
                link(V.tensor_scalar(eight[:, 0:2], place[:], CAP - 0.5, None, ALU.is_gt), l)
                for n in (2, 3):
                    link(V.scalar_tensor_tensor(out=eight[:, 0:2], in0=place[:], scalar=CAP * n - 0.5, in1=eight[:, 0:2], op0=ALU.is_gt, op1=ALU.add), l)
                V.tensor_tensor(vid[:], vid[:], eight[:, 0:2], ALU.add)
                link(V.scalar_tensor_tensor(out=place[:], in0=eight[:, 0:2], scalar=-float(CAP), in1=place[:], op0=ALU.mult, op1=ALU.add), l)
                for t in range(TT):
                    V.tensor_scalar(one_hot[:, t, :], iota, place[:, t:t + 1], None, ALU.is_equal)
                for t in range(TT):
                    link(V.tensor_scalar(vmask[:, t, :], iota[:, 0:MAX_VISITS + 1], vid[:, t:t + 1], None, ALU.is_equal), l)

                def fill_slots(n):
                    for t in range(TT):
                        ins = V.tensor_scalar(slots1[:, t, :], one_hot[:, t, :], vmask[:, t, bass.ds(n, 1)], None, ALU.mult)
                    ins.then_inc(ev("slots_ready"), 1)
                fill_slots(done)
                dv.wait_ge(ev("visits_counted"), l + 2)
                end = dv.value_load(visits[0:1, bass.ds(l * NG + NG, 1)], min_val=0, max_val=MAX_VISITS)

                with dv.Fori(done, end) as v:
                    dv.wait_ge(ev("gathered"), v + 1)
                    V.tensor_copy(hg.rearrange("p k s -> p (k s)"), psum[0][:, 0:KD * CAP]).then_inc(ev("hg_ready"), 1)
                    dv.wait_ge(ev("slots_used"), v + 1)
                    for j in range(2):
                        r = CAP * j
                        V.tensor_copy(wsel[r:r + CAP, :], psum[2][r:r + CAP, 0:EG].rearrange("p (e r) -> p e r", r=2)[:, :, j]).then_inc(ev("wsel_ready"), 1)
                    dv.wait_ge(ev("slots_ready"), v + l + 1)
                    fill_slots(v + 1)
                    dv.wait_ge(ev("wsel_ready"), v * 2 + 2)
                    for r in range(2):
                        dv.wait_ge(ev("silu_ready"), v * 2 + (r + 1))
                        V.scalar_tensor_tensor(out=he[:, r, :], in0=psum[1][:, 512 * r + FF:512 * r + 2 * FF], scalar=wsel[:, r:r + 1],
                                               in1=silu_g[:, r, :], op0=ALU.mult, op1=ALU.mult).then_inc(ev("he_ready"), 1)
                    dv.wait_ge(ev("down_done"), v * 2 + 4)
                    V.tensor_copy(yslot[:, 512:1024], psum[2][:, 512:1024]).then_inc(ev("yslot_ready"), 1)
                    for i in range(2):
                        dv.wait_ge(ev("scattered"), v * 2 + (i + 1))
                        for j in range(4):
                            k = 4 * i + j
                            ins = V.scalar_tensor_tensor(out=xT[:, k, :], in0=psum[3 - 2 * i][:, j * S:(j + 1) * S], scalar=mod[:, 40 + k:41 + k],
                                                         in1=xT[:, k, :], op0=ALU.mult, op1=ALU.add)
                        ins.then_inc(ev("scatter_added"), 1)
                    dv.wait_ge(ev("scatter_added"), v * 2 + 3)
                assert chain[0] == first + K_DVE, chain[0] - first

            dv.wait_ge(ev("final_sum"), 1)
            V.tensor_scalar(var[:], psum[0][:, 0:S], 1.0 / D, EPS, ALU.mult, ALU.add).then_inc(ev("var3"), 1)
            dv.wait_ge(ev("root3"), 1)
            V.reciprocal(var[:], rstd[:]).then_inc(ev("final_rstd"), 1)
            dv.wait_ge(ev("final_rstd"), 1)
            V.tensor_tensor(hT[:], xT[:], var[:].unsqueeze(1).broadcast_to([P, KD, S]), ALU.mult).then_inc(ev("final_rstd"), 1)
            dv.wait_ge(ev("final_rstd"), 2)
            for k in range(KD):
                ins = V.tensor_scalar(hT[:, k, :], hT[:, k, :], pcol[:, 40 + k:41 + k], None, ALU.mult)
            ins.then_inc(ev("final_ready"), 1)


NFIRST = 7
NSMALL = 5


_INS = ["x", "c", "positions", "norm_attn_g", "norm_ffn_g", "w_ada", "b_ada", "w_in", "hgrn_lb_logits", "hgrn_norm_g",
        "attn_sinks", "w_branch_a", "w_branch_b", "w_branch_c", "w_out", "router_w", "router_b", "w_gate", "w_up",
        "w_down", "final_norm_g"]


def kernel(**inputs):
    import concourse.bacc as bacc
    from concourse.bass_utils import run_bass_kernel_spmd

    nc = bacc.Bacc("TRN2", target_bir_lowering=False, num_devices=1)
    arrays, aps = {}, {}
    given = {name: np.ascontiguousarray(inputs[name]) for name in _INS}
    given["constants"], given["level_masks"] = constants()
    for name, x in given.items():
        arrays[f"in_{name}"] = x
        aps[name] = nc.dram_tensor(f"in_{name}", x.shape, mybir.dt.from_np(x.dtype), kind="ExternalInput").ap()
    out = nc.dram_tensor("out_0", (1, S, D), F32, kind="ExternalOutput").ap()
    trunk(nc, aps, out)
    r = run_bass_kernel_spmd(nc, [arrays], core_ids=[0])
    return r.results[0]["out_0"]
```
